# Optimizing a Trainium2 kernel written in Bass

```python
import math
import jax, jax.numpy as jnp
from jax import lax
import numpy as np

D_MODEL = 1024
BATCH = 1
SEQ = 512
DEPTH = 2

N_MIXERS = 2
N_RWKV_LAYERS = (DEPTH + N_MIXERS - 1) // N_MIXERS
N_DIFF_LAYERS = DEPTH // N_MIXERS
NORM_EPS = 1e-6

RW_HEAD = 64
RW_HEADS = D_MODEL // RW_HEAD
RW_WIDTH = RW_HEADS * RW_HEAD
RW_N_PROJ = 4
RW_N_MIX = 6
DECAY_LORA = max(32, int(round(1.8 * D_MODEL ** 0.5 / 32)) * 32)
ICLR_LORA = max(32, int(round(1.8 * D_MODEL ** 0.5 / 32)) * 32)
GN_EPS = 64e-5

DA_HEADS = 8
DA_QK_DIM = D_MODEL // DA_HEADS // 2
DA_V_DIM = 2 * DA_QK_DIM
DA_WIDTH = DA_HEADS * DA_V_DIM
DA_SUBLN_EPS = 1e-5
ROPE_THETA = 10000.0
Q_BLOCK = 128

PLE_DIM = 256


def rms_norm(x, g, eps=NORM_EPS):
    xf = x.astype(jnp.float32)
    y = xf * lax.rsqrt(jnp.mean(xf * xf, axis=-1, keepdims=True) + eps)
    return (y * g.astype(jnp.float32)).astype(x.dtype)

def token_shift(x):
    return jnp.pad(x, ((0, 0), (1, 0), (0, 0)))[:, :-1]

def rwkv7_mixer(h, mu, w_in, w0, w1, w2, a0, a1, a2, k_k, k_a, r_k, ln_w, ln_b, w_out):
    B, S, _ = h.shape
    H, N = RW_HEADS, RW_HEAD
    f32 = jnp.float32
    dx = token_shift(h) - h
    xm = h[:, :, None, :] + dx[:, :, None, :] * mu[:RW_N_PROJ]
    proj = jnp.einsum('bsgd,dgc->bsgc', xm, w_in.reshape(D_MODEL, RW_N_PROJ, RW_WIDTH))
    r, k, v, gate = proj[:, :, 0], proj[:, :, 1], proj[:, :, 2], proj[:, :, 3]
    xw = h + dx * mu[4]
    xa = h + dx * mu[5]
    w_log = -jax.nn.softplus(-(w0 + jnp.tanh(xw @ w1) @ w2).astype(f32)) - 0.5
    decay = jnp.exp(-jnp.exp(w_log))
    a = jax.nn.sigmoid((a0 + (xa @ a1) @ a2).astype(f32))
    kk = (k * k_k).reshape(B, S, H, N).astype(f32)
    kk = kk / jnp.maximum(jnp.sqrt(jnp.sum(kk * kk, axis=-1, keepdims=True)), 1e-12)
    k = k.astype(f32) * (1.0 + (a - 1.0) * k_a.astype(f32))

    def heads(t):
        return t.reshape(B, S, H, N).astype(f32)

    rh, kh, vh, wh, ah = heads(r), heads(k), heads(v), heads(decay), heads(a)
    bh = kk * ah

    def step(state, inp):
        r_t, w_t, k_t, v_t, kk_t, b_t = inp
        sa = jnp.einsum('bhij,bhj->bhi', state, kk_t)
        state = (state * w_t[:, :, None, :] - sa[..., None] * b_t[:, :, None, :]
                 + v_t[..., None] * k_t[:, :, None, :])
        y_t = jnp.einsum('bhij,bhj->bhi', state, r_t)
        return state, y_t

    seq_first = lambda t: jnp.swapaxes(t, 0, 1)
    s0 = jnp.zeros((B, H, N, N), f32)
    _, y = lax.scan(step, s0, (seq_first(rh), seq_first(wh), seq_first(kh),
                               seq_first(vh), seq_first(kk), seq_first(bh)))
    y = jnp.swapaxes(y, 0, 1)
    mean = jnp.mean(y, axis=-1, keepdims=True)
    var = jnp.mean(jnp.square(y - mean), axis=-1, keepdims=True)
    y = ((y - mean) * lax.rsqrt(var + GN_EPS) * ln_w.reshape(H, N).astype(f32)
         + ln_b.reshape(H, N).astype(f32))
    bonus = jnp.sum(rh * kh * r_k.astype(f32), axis=-1, keepdims=True) * vh
    y = (y + bonus).reshape(B, S, RW_WIDTH).astype(h.dtype)
    return (y * jax.nn.silu(gate)) @ w_out

def rope(x, cos, sin):
    half = x.shape[-1] // 2
    x1, x2 = x[..., :half], x[..., half:]
    rot = jnp.concatenate([-x2, x1], axis=-1)
    return (x * cos + rot * sin).astype(x.dtype)

def diff_attn_mixer(h, w_in, lq1, lk1, lq2, lk2, subln, w_out, lambda_init):
    B, S, _ = h.shape
    H, dk, dv = DA_HEADS, DA_QK_DIM, DA_V_DIM
    f32 = jnp.float32
    nb = S // Q_BLOCK
    proj = h @ w_in
    q, k, v, gate = jnp.split(proj, [2 * H * dk, 4 * H * dk, 4 * H * dk + H * dv], axis=-1)
    q = q.reshape(B, S, H, 2, dk)
    k = k.reshape(B, S, H, 2, dk)
    v = v.reshape(B, S, H, dv)
    pos = jnp.arange(S, dtype=f32)
    inv_freq = 1.0 / (ROPE_THETA ** (jnp.arange(0, dk, 2, dtype=f32) / dk))
    ang = pos[:, None] * inv_freq[None, :]
    ang = jnp.concatenate([ang, ang], axis=-1)
    cos = jnp.cos(ang)[:, None, None, :]
    sin = jnp.sin(ang)[:, None, None, :]
    q = rope(q, cos, sin)
    k = rope(k, cos, sin)
    lam = (jnp.exp(jnp.sum(lq1.astype(f32) * lk1.astype(f32)))
           - jnp.exp(jnp.sum(lq2.astype(f32) * lk2.astype(f32))) + lambda_init)
    scale = dk ** -0.5
    qb = q.reshape(B, nb, Q_BLOCK, H, 2, dk).transpose(1, 0, 3, 4, 2, 5)
    kt = k.transpose(0, 2, 3, 1, 4)
    vt = v.transpose(0, 2, 1, 3)
    key_pos = jnp.arange(S)

    def block(args):
        i, qi = args
        s = jnp.einsum('bhcqd,bhckd->bhcqk', qi, kt).astype(f32) * scale
        q_pos = i * Q_BLOCK + jnp.arange(Q_BLOCK)
        s = jnp.where(key_pos[None, :] <= q_pos[:, None], s, -jnp.inf)
        pr = jax.nn.softmax(s, axis=-1)
        att = pr[:, :, 0] - lam * pr[:, :, 1]
        return jnp.einsum('bhqk,bhkd->bhqd', att.astype(vt.dtype), vt)

    o = lax.map(block, (jnp.arange(nb), qb))
    o = o.transpose(1, 0, 3, 2, 4).reshape(B, S, H, dv)
    o = rms_norm(o, subln, DA_SUBLN_EPS) * (1.0 - lambda_init)
    o = o.reshape(B, S, DA_WIDTH)
    return (o * jax.nn.silu(gate)) @ w_out

def first_inputs(seed: int = 0) -> dict:
    key = jax.random.key(seed)
    ks = iter(jax.random.split(key, 40))
    nrm = lambda shape, s: jax.random.normal(next(ks), shape, jnp.float32) * s
    NA, NB, D, C = N_RWKV_LAYERS, N_DIFF_LAYERS, D_MODEL, RW_WIDTH
    lin = jnp.linspace(0.0, 1.0, C, dtype=jnp.float32)
    return {
        'x': nrm((BATCH, SEQ, D), 1.0),
        'p': nrm((DEPTH, BATCH, SEQ, PLE_DIM), 1.0),
        'rw_norm': 1.0 + nrm((NA, D), 0.05),
        'rw_mu': jax.random.uniform(next(ks), (NA, RW_N_MIX, D), jnp.float32),
        'rw_w_in': nrm((NA, D, RW_N_PROJ * C), D ** -0.5),
        'rw_w0': (-7.0 + 5.0 * lin ** 0.85 + 0.5)[None, :] + nrm((NA, C), 0.1),
        'rw_w1': nrm((NA, D, DECAY_LORA), D ** -0.5),
        'rw_w2': nrm((NA, DECAY_LORA, C), 0.1 * DECAY_LORA ** -0.5),
        'rw_a0': nrm((NA, C), 0.1),
        'rw_a1': nrm((NA, D, ICLR_LORA), D ** -0.5),
        'rw_a2': nrm((NA, ICLR_LORA, C), 0.3 * ICLR_LORA ** -0.5),
        'rw_k_k': 0.85 + nrm((NA, C), 0.05),
        'rw_k_a': 1.0 + nrm((NA, C), 0.05),
        'rw_r_k': nrm((NA, RW_HEADS, RW_HEAD), 0.1),
        'rw_ln_w': 1.0 + nrm((NA, C), 0.05),
        'rw_ln_b': nrm((NA, C), 0.02),
        'rw_w_out': nrm((NA, C, D), C ** -0.5),
        'da_norm': 1.0 + nrm((NB, D), 0.05),
        'da_w_in': nrm((NB, D, 4 * DA_HEADS * DA_QK_DIM + 2 * DA_WIDTH), D ** -0.5),
        'da_lq1': nrm((NB, DA_QK_DIM), 0.1),
        'da_lk1': nrm((NB, DA_QK_DIM), 0.1),
        'da_lq2': nrm((NB, DA_QK_DIM), 0.1),
        'da_lk2': nrm((NB, DA_QK_DIM), 0.1),
        'da_subln': 1.0 + nrm((NB, DA_V_DIM), 0.05),
        'da_w_out': nrm((NB, DA_WIDTH, D), DA_WIDTH ** -0.5),
        'pe_norm': 1.0 + nrm((DEPTH, D), 0.05),
        'pe_w_gate': nrm((DEPTH, D, D), D ** -0.5),
        'pe_w_proj': nrm((DEPTH, PLE_DIM, D), PLE_DIM ** -0.5),
        'final_norm': 1.0 + nrm((D,), 0.05),
    }

def first_block(x, p, rw_norm, rw_mu, rw_w_in, rw_w0, rw_w1, rw_w2, rw_a0, rw_a1, rw_a2,
              rw_k_k, rw_k_a, rw_r_k, rw_ln_w, rw_ln_b, rw_w_out,
              da_norm, da_w_in, da_lq1, da_lk1, da_lq2, da_lk2, da_subln, da_w_out,
              pe_norm, pe_w_gate, pe_w_proj, final_norm):
    h = x
    for i in range(DEPTH):
        j = i // N_MIXERS
        if i % N_MIXERS == 0:
            h = h + rwkv7_mixer(rms_norm(h, rw_norm[j]), rw_mu[j], rw_w_in[j], rw_w0[j], rw_w1[j],
                                rw_w2[j], rw_a0[j], rw_a1[j], rw_a2[j], rw_k_k[j], rw_k_a[j],
                                rw_r_k[j], rw_ln_w[j], rw_ln_b[j], rw_w_out[j])
        else:
            lambda_init = 0.8 - 0.6 * math.exp(-0.3 * i)
            h = h + diff_attn_mixer(rms_norm(h, da_norm[j]), da_w_in[j], da_lq1[j], da_lk1[j],
                                    da_lq2[j], da_lk2[j], da_subln[j], da_w_out[j], lambda_init)
        g = jax.nn.sigmoid(rms_norm(h, pe_norm[i]) @ pe_w_gate[i])
        h = h + g * (p[i] @ pe_w_proj[i])
    return rms_norm(h, final_norm)


N_A_LAYERS = DEPTH // 2
N_B_LAYERS = DEPTH - N_A_LAYERS
CONV_WIDTH = 3
N_HEADS = 8
HEAD_DIM = 64
ATT_WIDTH = N_HEADS * HEAD_DIM
RMS_EPS = 1e-6


def _rmsnorm(x, g):
    xf = x.astype(jnp.float32)
    y = xf * lax.rsqrt(jnp.mean(xf * xf, axis=-1, keepdims=True) + RMS_EPS)
    return (y * g.astype(jnp.float32)).astype(x.dtype)

def _causal_depthwise_conv(u, w):
    return lax.conv_general_dilated(
        u, w[:, None, :].astype(u.dtype),
        window_strides=(1,),
        padding=[(CONV_WIDTH - 1, 0)],
        dimension_numbers=("NWC", "WIO", "NWC"),
        feature_group_count=u.shape[-1])

def _short_conv_mixer(h, w_in, w_conv, w_out):
    u = h @ w_in
    b_gate, c_gate, xin, g = jnp.split(u, 4, axis=-1)
    y = b_gate * _causal_depthwise_conv(c_gate * xin, w_conv)
    return (y * jax.nn.silu(g)) @ w_out

def _stick_breaking_attention(q, k, v):
    seq = q.shape[2]
    n_blocks = seq // Q_BLOCK
    scale = HEAD_DIM ** -0.5
    qf = q.astype(jnp.float32)
    kf = k.astype(jnp.float32)
    vf = v.astype(jnp.float32)
    outs = []
    for blk in range(n_blocks):
        q0 = blk * Q_BLOCK
        kl = q0 + Q_BLOCK
        qb = qf[:, :, q0:kl]
        z = jnp.einsum("bhqd,bhkd->bhqk", qb, kf[:, :, :kl]) * scale
        q_pos = q0 + jnp.arange(Q_BLOCK)
        mask = jnp.arange(kl)[None, :] < q_pos[:, None]
        log_one_minus = jnp.where(mask, jax.nn.log_sigmoid(-z), 0.0)
        rev = lax.cumsum(log_one_minus, axis=3, reverse=True)
        weights = jnp.exp(jnp.where(mask, z + rev, -jnp.inf))
        outs.append(jnp.einsum("bhqk,bhkd->bhqd", weights, vf[:, :, :kl]))
    o = jnp.concatenate(outs, axis=2)
    return o.astype(q.dtype)

def second_inputs(seed: int = 0) -> dict:
    key = jax.random.key(seed)
    ks = jax.random.split(key, 12)
    D = D_MODEL
    s = D ** -0.5
    f32 = jnp.float32
    return {
        "x": jax.random.normal(ks[0], (BATCH, SEQ, D), f32),
        "norm_a": 1.0 + 0.02 * jax.random.normal(ks[1], (N_A_LAYERS, D), f32),
        "w_in_a": s * jax.random.normal(ks[2], (N_A_LAYERS, D, 4 * D), f32),
        "conv_a": (CONV_WIDTH ** -0.5) * jax.random.normal(ks[3], (N_A_LAYERS, CONV_WIDTH, D), f32),
        "w_out_a": s * jax.random.normal(ks[4], (N_A_LAYERS, D, D), f32),
        "norm_kv": 1.0 + 0.02 * jax.random.normal(ks[5], (D,), f32),
        "w_kv": s * jax.random.normal(ks[6], (D, 2 * ATT_WIDTH), f32),
        "norm_b": 1.0 + 0.02 * jax.random.normal(ks[7], (N_B_LAYERS, D), f32),
        "w_in_b": s * jax.random.normal(ks[8], (N_B_LAYERS, D, 2 * ATT_WIDTH), f32),
        "w_out_b": (ATT_WIDTH ** -0.5) * jax.random.normal(ks[9], (N_B_LAYERS, ATT_WIDTH, D), f32),
        "norm_f": 1.0 + 0.02 * jax.random.normal(ks[10], (D,), f32),
    }

def second_block(x, norm_a, w_in_a, conv_a, w_out_a, norm_kv, w_kv, norm_b, w_in_b, w_out_b, norm_f):
    bsz, seq, _ = x.shape
    k = v = None
    for layer in range(DEPTH):
        if layer < N_A_LAYERS:
            i = layer
            h = _rmsnorm(x, norm_a[i])
            x = x + _short_conv_mixer(h, w_in_a[i], conv_a[i], w_out_a[i])
            if layer == N_A_LAYERS - 1:
                kv = _rmsnorm(x, norm_kv) @ w_kv
                k, v = jnp.split(kv, 2, axis=-1)
                k = k.reshape(bsz, seq, N_HEADS, HEAD_DIM).transpose(0, 2, 1, 3)
                v = v.reshape(bsz, seq, N_HEADS, HEAD_DIM).transpose(0, 2, 1, 3)
        else:
            j = layer - N_A_LAYERS
            h = _rmsnorm(x, norm_b[j])
            q, g = jnp.split(h @ w_in_b[j], 2, axis=-1)
            q = q.reshape(bsz, seq, N_HEADS, HEAD_DIM).transpose(0, 2, 1, 3)
            o = _stick_breaking_attention(q, k, v)
            o = o.transpose(0, 2, 1, 3).reshape(bsz, seq, ATT_WIDTH)
            x = x + (o * jax.nn.silu(g)) @ w_out_b[j]
    return _rmsnorm(x, norm_f)


def setup_inputs(seed=0):
    out = dict(first_inputs(seed))
    for name, value in second_inputs(seed + 1).items():
        if name != "x":
            out[name + "_2"] = value
    return out


def reference(
    x, p, rw_norm, rw_mu, rw_w_in, rw_w0, rw_w1, rw_w2, rw_a0, rw_a1, rw_a2, rw_k_k, rw_k_a,
    rw_r_k, rw_ln_w, rw_ln_b, rw_w_out, da_norm, da_w_in, da_lq1, da_lk1, da_lq2, da_lk2,
    da_subln, da_w_out, pe_norm, pe_w_gate, pe_w_proj, final_norm, norm_a_2, w_in_a_2, conv_a_2,
    w_out_a_2, norm_kv_2, w_kv_2, norm_b_2, w_in_b_2, w_out_b_2, norm_f_2,
):
    x = first_block(
        x, p, rw_norm, rw_mu, rw_w_in, rw_w0, rw_w1, rw_w2, rw_a0, rw_a1, rw_a2, rw_k_k, rw_k_a,
        rw_r_k, rw_ln_w, rw_ln_b, rw_w_out, da_norm, da_w_in, da_lq1, da_lk1, da_lq2, da_lk2,
        da_subln, da_w_out, pe_norm, pe_w_gate, pe_w_proj, final_norm,
    )
    return second_block(
        x, norm_a_2, w_in_a_2, conv_a_2, w_out_a_2, norm_kv_2, w_kv_2, norm_b_2, w_in_b_2,
        w_out_b_2, norm_f_2,
    )


_drawn_inputs = setup_inputs


def setup_inputs(seed=0):
    import zlib

    import numpy as np

    out = dict(_drawn_inputs(seed))
    spreads = {}
    factors = {'rw_w1': 8.0,
     'rw_w2': 8.0,
     'rw_ln_b': 4.214,
     'da_lq1': 5.644,
     'da_lk1': 8.0,
     'da_lq2': 4.533,
     'da_lk2': 7.668,
     'pe_norm': 3.185,
     'norm_kv_2': 8.0,
     'norm_b_2': 7.831,
     'norm_f_2': 2.868}
    for name, (base, spread) in spreads.items():
        noise = np.random.default_rng([zlib.crc32(name.encode()), seed]).standard_normal(out[name].shape)
        drawn = base * np.exp(spread * noise) if base else spread * noise
        out[name] = __import__('jax').numpy.asarray(drawn.astype(out[name].dtype))
    for name, factor in factors.items():
        out[name] = (out[name] * factor).astype(out[name].dtype)
    return out
```

```python
import math
from contextlib import ExitStack

import numpy as np

import concourse.bass as bass
from concourse import mybir

P = 128
F32 = mybir.dt.float32
F32R = mybir.dt.float32r
ALU = mybir.AluOpType
ACT = mybir.ActivationFunctionType
AX = mybir.AxisListType

TOK = 512
DM = 1024
NT = DM // P
TT = TOK // P
CH = 64
NC = TOK // CH
BL = CH // 2
HEADS = DM // CH
LORA = 64
PLE = 256
SLOT = DM
NEG = -1.0e30
DECAY = math.exp(-0.5)
LAMBDA_INIT = 0.8 - 0.6 * math.exp(-0.3)
QK_SCALE = CH ** -0.5
NORM_EPS, GN_EPS, SUB_EPS = 1e-6, 64e-5, 1e-5

(G_RW, MU_R, MU_K, MU_V, MU_G, MU_W, MU_A, W0, A0, K_K, K_A, R_K, LN_W, LN_B, G_DA,
 G_PE0, G_PE1, G_FIRST, G_CONV, CONV0, CONV1, CONV2, G_KV, G_B, G_LAST, SUBLN) = range(26)
PARAM_ROWS = SUBLN * NT + 1
PRM_DMAS = 19

CONST_COLS = {}
_at = 0
for _name, _w in (("ident", P), ("ones", P), ("center", P), ("causal_add", P), ("strict_add", P),
                  ("strict_mul", P), ("strict_x", P), ("strict_s", CH), ("diagonal", P), ("between", P), ("incl_s", CH), ("head_of", NT * HEADS),
                  ("tile_of", NT * NT), ("eps", 4)):
    CONST_COLS[_name] = (_at, _at + _w)
    _at += _w
CONST_W = _at


def constant_tables():
    q, k = np.meshgrid(np.arange(P), np.arange(P), indexing="ij")
    half = (q // CH) == (k // CH)
    s, t = np.arange(P)[:, None] % CH, np.arange(CH)[None, :]
    head_of = np.zeros((P, NT, HEADS))
    tile_of = np.zeros((P, NT, NT))
    for j in range(NT):
        tile_of[:, j, j] = 1.0
        for p in range(P):
            head_of[p, j, 2 * j + p // CH] = 1.0
    eps = np.tile(np.array([NORM_EPS, GN_EPS, SUB_EPS, 1.0]), (P, 1))
    parts = [np.eye(P), np.ones((P, P)), np.eye(P) - half / CH, np.where(k <= q, 0.0, NEG),
             np.where(k < q, 0.0, NEG), (k < q) * 1.0, ((k % CH) > (q % CH)) * half * 1.0, (t > s) * 1.0,
             ((k // BL) == (q // BL)) * 1.0, half * ((k // BL) == (q // BL) + 1) * 1.0, (t >= s) * 1.0,
             head_of.reshape(P, -1), tile_of.reshape(P, -1), eps]
    consts = np.concatenate(parts, axis=1).astype(np.float32)
    assert consts.shape == (P, CONST_W)
    head_rows = np.ascontiguousarray(head_of.transpose(2, 1, 0)).astype(np.float32)
    tile_rows = np.ascontiguousarray(tile_of.transpose(2, 1, 0)).astype(np.float32)
    freq = (1.0 / (10000.0 ** (np.arange(0, CH, 2, dtype=np.float32) / np.float32(CH)))).astype(np.float32)
    ang = (np.arange(TOK, dtype=np.float32)[:, None] * freq[None, :]).astype(np.float32)
    ang = np.concatenate([ang, ang], axis=1)
    sign = np.where(np.arange(CH) < CH // 2, -1.0, 1.0)
    cos = np.tile(np.cos(ang).T, (2, 1))
    sin = np.tile((np.sin(ang) * sign[None, :]).T, (2, 1))
    rope = np.stack([cos, sin], axis=1).astype(np.float32)
    keep = np.ones((P, TOK), np.float32)
    keep[:, ::CH] = 0.0
    return {"consts": consts, "head_rows": head_rows, "tile_rows": tile_rows,
            "rope_table": np.ascontiguousarray(rope), "keep": keep}


RUN_PLE = (0, 0)
RUN_K, RUN_R, RUN_V, RUN_GATE = (4, 16), (12, 24), (20, 32), (28, 40)
RUN_RWO, RUN_PE0 = (36, 48), (44, 56)
RUN_DQ, RUN_DK, RUN_DV, RUN_DG = (52, 64), (60, 72), (68, 80), (76, 88)
RUN_DAO, RUN_PE1 = (84, 96), (92, 104)
RUN_CC, RUN_CX, RUN_CB, RUN_CG = (100, 112), (108, 120), (116, 128), (124, 136)
RUN_CO, RUN_KV, RUN_QG, RUN_BO = (132, 144), (140, 152), (148, 160), (156, 168)
SLOTS, OUTS = 160, 176
A_PLE, A_K, A_R, A_V, A_GATE, A_RWO, A_PE0, A_DA, A_DAO, A_PE1, A_CONV, A_CO, A_KV, A_QG, A_BO = (
    0, 4, 12, 20, 28, 36, 44, 52, 60, 68, 76, 84, 92, 100, 108)


def build(nc, a, out):
    with ExitStack() as ctx:
        emit(nc, ctx, a, out)


class Clock:

    def __init__(self, eng, sem):
        self.eng, self.sem, self.n, self.trip = eng, sem, 0, None

    def enter(self, trip, per_trip):
        self.trip, self.per, self.start = trip, per_trip, self.n

    def leave(self, trips):
        assert self.n - self.start == self.per, (self.n - self.start, self.per)
        self.n = self.start + trips * self.per
        self.trip = None

    def step(self, ins):
        ins.then_inc(self.sem, 1)
        self.n += 1
        self.eng.wait_ge(self.sem, self.n if self.trip is None else self.trip * self.per + self.n)


def row(buf, j):
    return buf[:, j, :] if isinstance(j, int) else buf[:, bass.ds(j, 1), :]


def emit(nc, ctx, a, out):
    base = (nc.sbuf_base + 31) // 32 * 32
    at = [0]

    def place(name, shape, dtype, offset):
        size = int(np.prod(shape[1:])) * 4
        assert base + offset + size <= nc.sbuf_usable_end, (name, offset + size)
        return nc.alloc_sbuf_tensor_at("b_" + name, list(shape), dtype, offset=base + offset)

    def resident(name, shape, dtype=F32):
        t = place(name, shape, dtype, at[0])
        at[0] += (int(np.prod(shape[1:])) * 4 + 31) // 32 * 32
        return t

    CST = resident("consts", [P, CONST_W])
    PRM = resident("params", [P, 256])
    STAT_KA = PRM[:, 216:216 + NT]
    WRAW = resident("w_raw", [P, 4, NT, P])
    WHI = resident("w_hi", [P, 2, NT, P], F32R)
    WLO = resident("w_lo", [P, 2, NT, P], F32R)
    a_at = at[0]
    AHI = resident("a_hi", [P, NT, TOK], F32R)
    ALO = resident("a_lo", [P, NT, TOK], F32R)
    XT = resident("x_t", [P, NT, TOK])
    RB = resident("rstd", [P, TOK])
    SQ = resident("squares", [P, 2, TOK])
    ACC = resident("sum_squares", [P, TOK])
    arena = at[0]
    FULL = NT * TOK * 4

    def phase(entries, start=0):
        o, made = arena + start, []
        for name, shape in entries:
            made.append(place(name, shape, F32, o))
            o += (int(np.prod(shape[1:])) * 4 + 31) // 32 * 32
        return made

    H, DX, KT, RT, KH, NB, TMP, HEADROWS, KEEP, RK, PC = phase([
        ("h_t", [P, NT, TOK + 1]), ("dx", [P, NT, TOK]), ("k_tilde", [P, NT, TOK]), ("r_tilde", [P, NT, TOK]),
        ("k_hat", [P, NT, TOK]), ("n_b", [P, NT, TOK]), ("rw_tmp", [P, 4, TOK]), ("head_rows", [HEADS, NT, P]),
        ("keep_state", [P, TOK]), ("head_sums", [HEADS, TOK]),
        ("chunk_decay", [P, NC, NT])])
    h_size = NT * (TOK + 1) * 4
    kt_at, rt_at, kh_at, nb_at = (h_size + (1 + n) * FULL for n in range(4))
    LW1 = place("lora_w1", [P, 2, NT, LORA], F32, a_at + FULL + FULL // 2)
    LW2 = place("lora_w2", [LORA, 2, DM], F32, a_at + FULL // 2)
    (XROWS,) = phase([("x_rows", [P, TT, DM])], kh_at)
    PROWS, PRMROWS = phase([("p_rows", [P, 2, TT, PLE]), ("prm_rows", [P, 2, P])], nb_at)
    (PLEOUT,) = phase([("ple_out", [P, 4, TOK])], rt_at)
    (GT,) = phase([("gate_t", [P, NT, TOK])])
    (YT,) = phase([("y_t", [P, NT, TOK])], h_size)
    (PROB,) = phase([("problems", [P, CH, CH])], kt_at + 6 * 4096)
    NBX, KTX, KHX, KRC, VTX, TTX, KS, VX, AKX, RC, WX, UX, STX = phase([
        ("nb_x", [P, 2, NT, P]), ("kt_x", [P, 2, NT, P]), ("kh_x", [P, 2, NT, P]), ("kr_c", [P, 2, NT, 2, CH]),
        ("vt_x", [P, 2, NT, P]), ("tt_x", [P, 2, NT, P]), ("k_rows", [P, 2, NT, P]), ("v_rows", [P, NT, P]),
        ("ak_x", [P, NT, P]), ("r_c", [P, NT, 2, CH]), ("w_x", [P, NT, P]), ("u_x", [P, NT, P]),
        ("state_x", [P, NT, P])], kt_at)
    BDIAG, BETW = (WX[:, :, :], UX[:, :, :], AKX[:, :, :], VX[:, :, :]), (KS[:, 0], KS[:, 1])
    BDIAGT, BPROD = (KHX[:, 0], KHX[:, 1]), (NBX[:, 0], NBX[:, 1])
    KTC, NA, OUTER = phase([("kt_c", [P, 2, NT, CH]), ("a_nb", [P, 2, NT, CH]), ("outer", [P, 2, (CH // 4) ** 2])],
                           kt_at + 17 * 4096)
    TALL = place("t_all", [P, NC, NT, P], F32, a_at)
    BVT, HEADROWS2, RK2, YTMP = phase([("bonus_v", [P, NT, TOK]), ("head_rows2", [HEADS, NT, P]),
                                       ("gn_rstd", [HEADS, TOK]), ("gn_tmp", [P, 2, TOK])], kt_at)
    PP, PTMP = phase([("ple_in", [P, NT, TOK]), ("ple_tmp", [P, 2, TOK])])
    (DQT, DKT, DV, DGT, ROPE, RTMP, VSTAGE, QS, KSD, VS, ES, ATT, ATTT, STAT, TILEROWS, RK8) = phase([
        ("dq_t", [P, NT, TOK]), ("dk_t", [P, NT, TOK]), ("dv_rows", [P, TT, DM]), ("dg_t", [P, NT, TOK]),
        ("rope", [P, 2, TOK]), ("rope_tmp", [P, 3, TOK]), ("v_stage", [P, 2, TOK]), ("q_head", [P, 2, TOK]),
        ("k_head", [P, 2, TOK]), ("v_head", [P, 2, TT, P]), ("exps", [P, 2, 2, TOK]), ("att", [P, 2, TOK]),
        ("att_t", [P, 2, TOK]), ("stats", [P, 3, 16]), ("tile_rows", [NT, NT, P]), ("head_rstd8", [NT, TOK])])
    LQ = RTMP[:, 2, 0:4 * CH].rearrange("p (n d) -> p n d", d=CH)
    CU, CV, CTMP = phase([("conv_u", [P, NT, TOK + 2]), ("conv_v", [P, NT, TOK]), ("conv_tmp", [P, 4, TOK])])
    HT4 = NT // 2
    (SQT, SKT, SV, SGT, SVST, SQH, SKH, SVH, SAB, SSP, SSUF, SATT, SATTT) = phase([
        ("sq_t", [P, HT4, TOK]), ("sk_t", [P, HT4, TOK]), ("sv_rows", [P, TT, TOK]), ("sg_t", [P, HT4, TOK]),
        ("sv_stage", [P, 2, TOK]), ("sq_head", [P, 2, TOK]), ("sk_head", [P, 2, TOK]), ("sv_head", [P, 2, TT, P]),
        ("z_abs", [P, 2, 2, TOK]), ("softplus", [P, 2, 2, TOK]), ("suffix", [P, 2, 2, TOK]),
        ("weights", [P, 2, 2, TOK]), ("weights_t", [P, 2, 2, TOK])])
    FT, OROWS = phase([("final_t", [P, 2, TOK]), ("out_rows", [P, TT, DM])])

    PS = ctx.enter_context(nc.psum_tensor("banks", [P, 8, TOK], F32))
    BANK = [PS[:, n, :] for n in range(8)]
    made = {}

    def sem(name):
        if name not in made:
            made[name] = ctx.enter_context(nc.semaphore(name))
        return made[name]

    def dram(name, shape):
        return nc.dram_tensor(name, list(shape), F32, kind="Internal").ap()

    D_PLE = dram("d_ple", [2, NT, P, TOK])
    D_BV = dram("d_bonus_v", [NT, P, TOK])
    D_KT, D_RT, D_KH, D_NB, D_VT = (dram("d_" + n, [NC, P, NT, CH]) for n in ("kt", "rt", "kh", "nb", "vt"))
    D_A, D_T = (dram("d_" + n, [NC, NT, 2, CH, CH]) for n in ("a", "t"))

    def cst(name):
        lo, hi = CONST_COLS[name]
        return CST[:, lo:hi]

    IDENT, ONES = cst("ident"), cst("ones")
    HEADOF = cst("head_of").rearrange("p (j h) -> p j h", j=NT)
    TILEOF = cst("tile_of").rearrange("p (j h) -> p j h", j=NT)
    eps_at = CONST_COLS["eps"][0]

    def eps(n):
        return CST[:, eps_at + n:eps_at + n + 1]

    def prm(g, j=0):
        c = g * NT + j
        return PRM[:, c:c + 1] if isinstance(c, int) else PRM[:, bass.ds(c, 1)]

    block = ctx.enter_context(nc.Block())

    def outs_after(g):
        return 4 * (g + 1) if g < 4 else g + 13 if g < 156 else 168 + 2 * (g - 155)

    @block.sync
    def _(sp):
        def weights(tensor, g0, groups, col0=0, width=P, kt=NT):
            src = tensor.rearrange("(k p) n -> p k n", p=P)

            def four(trip):
                for u in range(4):
                    if g0 >= 4:
                        sp.wait_ge(sem("lo_done"), trip * 4 + (g0 + u - 3))
                    cols = bass.ds((trip * 4 + u) * width + col0, width)
                    dst = WRAW[:, u].rearrange("p k n -> p (k n)").rearrange("p (k n) -> p k n", k=kt)
                    sp.dma_start(dst, src[:, :, cols]).then_inc(sem(f"w_landed{u}"), 16)

            if groups == 1:
                four(0)
            else:
                with sp.Fori(0, groups) as trip:
                    four(trip)

        sp.dma_start(PROWS[:, :, :, :], a["p"].rearrange("l b (t p) d -> p (l b) t d", p=P)).then_inc(sem("p_in"), 16)
        sp.dma_start(CST[:, :], a["consts"]).then_inc(sem("consts_in"), 16)
        for layer in range(2):
            for u in range(2):
                dst = WRAW[:, 2 * layer + u].rearrange("p k n -> p (k n)").rearrange("p (k n) -> p k n", k=2)
                src = a["pe_w_proj"][layer].rearrange("(k p) n -> p k n", p=P)
                sp.dma_start(dst, src[:, :, u * TOK:(u + 1) * TOK]).then_inc(sem(f"w_landed{2 * layer + u}"), 16)
        for t in range(TT):
            sp.dma_start(XROWS[:, t, :], a["x"][0, t * P:(t + 1) * P, :]).then_inc(sem("x_in"), 16)
        for n, name in enumerate(("rw_w1", "rw_a1")):
            sp.dma_start(LW1[:, n], a[name][0].rearrange("(k p) n -> p k n", p=P)).then_inc(sem("lora_in"), 16)
        for n, name in enumerate(("rw_w2", "rw_a2")):
            sp.dma_start(LW2[:, n, :], a[name][0]).then_inc(sem("lora_in"), 16)
        sp.dma_start(KEEP[:, :], a["keep"]).then_inc(sem("tables_in"), 16)
        sp.dma_start(HEADROWS[:, :, :], a["head_rows"]).then_inc(sem("tables_in"), 16)
        win = a["rw_w_in"][0]
        weights(win, RUN_K[0], 2, 1 * DM)
        weights(win, RUN_R[0], 2, 0)
        weights(win, RUN_V[0], 2, 2 * DM)
        weights(win, RUN_GATE[0], 1, 3 * DM)

        sp.wait_ge(sem("spilled"), 16 * 4 * NC)
        sp.wait_ge(sem("zeroed"), 1)
        with sp.Fori(0, NC // 2) as i:
            for b in range(2):
                c = i * 2 + b
                sp.wait_ge(sem("a_mm"), c + 1)
                sp.dma_start(KTC[:, b], D_KT[bass.ds(c, 1)].rearrange("c p j t -> p (c j) t")).then_inc(sem(f"a_in{b}"), 16)
                for h in range(2):
                    sp.dma_start(NBX[h * CH:(h + 1) * CH, b, :, h * CH:(h + 1) * CH],
                                 D_NB[bass.ds(c, 1), h * CH:(h + 1) * CH].rearrange("c p j t -> p (c j) t")
                                 ).then_inc(sem(f"a_in{b}"), 16)
        for b in range(2):
            sp.wait_ge(sem(f"a_out{b}"), 16 * NC + 32)
        sp.dma_start(PROB[:, :, :], D_A.rearrange("c j h s t -> (c j h) s t")).then_inc(sem("prob_in"), 16)
        weights(win, RUN_GATE[0] + 4, 1, 3 * DM + DM // 2)
        weights(a["rw_w_out"][0], RUN_RWO[0], 1)
        sp.wait_ge(sem("inverse_done"), 1)
        sp.dma_start(D_T.rearrange("c j h s t -> (c j h) s t"), PROB[:, :, :]).then_inc(sem("t_out"), 16)
        sp.wait_ge(sem("t_out"), 16)
        sp.wait_ge(sem("zeroed"), 4)
        for c in range(NC):
            if c >= 2:
                sp.wait_ge(sem("diagonal_done"), c - 1)
                sp.wait_ge(sem("between_done"), c - 1)
            for h in range(2):
                hp = slice(h * CH, (h + 1) * CH)
                sp.dma_start(TTX[hp, c % 2, :, hp], D_T[c, :, h].rearrange("j s t -> s j t")
                             ).then_inc(sem(f"blocks_in{c % 2}"), 16)
        sp.wait_ge(sem("t_kept"), NC)
        sp.wait_ge(sem("zeroed"), 5)
        with sp.Fori(0, NC // 2) as i:
            for b in range(2):
                c = i * 2 + b
                sp.wait_ge(sem("y_mm"), c + 1)
                got = sem(f"chunk_in{b}")
                for h in range(2):
                    hp = slice(h * CH, (h + 1) * CH)
                    for dst, src in ((NBX, D_NB), (KTX, D_KT), (KHX, D_KH), (VTX, D_VT)):
                        sp.dma_start(dst[hp, b, :, hp], src[bass.ds(c, 1), hp].rearrange("c p j t -> p (c j) t")
                                     ).then_inc(got, 16)
                sp.dma_start(TTX[:, b], TALL[:, bass.ds(c, 1)].rearrange("p c j t -> p (c j) t")).then_inc(got, 16)
                for n, src in enumerate((D_KT, D_RT)):
                    sp.dma_start(KRC[:, b, :, n, :], src[bass.ds(c, 1)].rearrange("c p j t -> p (c j) t")
                                 ).then_inc(got, 16)
        sp.wait_ge(sem("y_done"), NC + 1)
        sp.wait_ge(sem("state_done"), 2 * NC + 2)
        sp.dma_start(BVT[:, :, :], D_BV.rearrange("j p t -> p j t")).then_inc(sem("gn_in"), 16)
        sp.dma_start(HEADROWS2[:, :, :], a["head_rows"]).then_inc(sem("gn_in"), 16)
        weights(a["rw_w_out"][0], RUN_RWO[0] + 4, 1, DM // 2)
        weights(a["pe_w_gate"][0], RUN_PE0[0], 1)
        sp.wait_ge(sem("act_ready"), A_RWO + NT)
        sp.dma_start(PP[:, :, :], D_PLE[0].rearrange("j p t -> p j t")).then_inc(sem("pp_in"), 16)
        sp.dma_start(ROPE[:, :, :], a["rope_table"]).then_inc(sem("da_in"), 16)
        sp.dma_start(TILEROWS[:, :, :], a["tile_rows"]).then_inc(sem("da_in"), 16)
        for n, name in enumerate(("da_lq1", "da_lk1", "da_lq2", "da_lk2")):
            sp.dma_start(LQ[:, n, :], a[name].to_broadcast([P, CH])).then_inc(sem("da_in"), 16)
        weights(a["pe_w_gate"][0], RUN_PE0[0] + 4, 1, DM // 2)
        win = a["da_w_in"][0]
        weights(win, RUN_DQ[0], 1)
        weights(win, RUN_DQ[0] + 4, 7, DM // 2)
        weights(a["da_w_out"][0], RUN_DAO[0], 1)
        sp.wait_ge(sem("rope_done"), 2 * NT + 1)
        sp.wait_ge(sem("v_turned"), NT + 2)
        with sp.Fori(0, NT // 2) as i:
            for b in range(2):
                j = i * 2 + b
                sp.wait_ge(sem("value_mm"), j * TT + TT)
                for dst, src in ((QS, DQT), (KSD, DKT)):
                    sp.dma_start(dst[:, b:b + 1, :], src[:, bass.ds(j, 1), :]).then_inc(sem(f"head_in{b}"), 16)
                sp.dma_start(VS[:, b], DV[:, :, bass.ds(j * P, P)]).then_inc(sem(f"head_in{b}"), 16)
        weights(a["da_w_out"][0], RUN_DAO[0] + 4, 1, DM // 2)
        weights(a["pe_w_gate"][1], RUN_PE1[0], 1)
        sp.wait_ge(sem("act_ready"), A_DAO + NT)
        sp.dma_start(PP[:, :, :], D_PLE[1].rearrange("j p t -> p j t")).then_inc(sem("pp_in"), 16)
        weights(a["pe_w_gate"][1], RUN_PE1[0] + 4, 1, DM // 2)
        win = a["w_in_a_2"][0]
        weights(win, RUN_CC[0], 2, 1 * DM)
        weights(win, RUN_CX[0], 2, 2 * DM)
        weights(win, RUN_CB[0], 2, 0)
        weights(win, RUN_CG[0], 2, 3 * DM)
        weights(a["w_out_a_2"][0], RUN_CO[0], 2)
        weights(a["w_kv_2"], RUN_KV[0], 2)
        weights(a["w_in_b_2"][0], RUN_QG[0], 2)
        weights(a["w_out_b_2"][0], RUN_BO[0], 1, 0, 2 * P, HT4)
        sp.wait_ge(sem("bank_free"), RUN_QG[1] + HT4)
        sp.wait_ge(sem("sv_turned"), HT4 + 2)
        with sp.Fori(0, HT4 // 2) as i:
            for b in range(2):
                j = i * 2 + b
                sp.wait_ge(sem("pair_mm"), j * TT + TT)
                for dst, src in ((SQH, SQT), (SKH, SKT)):
                    sp.dma_start(dst[:, b:b + 1, :], src[:, bass.ds(j, 1), :]).then_inc(sem(f"pair_in{b}"), 16)
                sp.dma_start(SVH[:, b], SV[:, :, bass.ds(j * P, P)]).then_inc(sem(f"pair_in{b}"), 16)
        for t in range(TT):
            sp.wait_ge(sem("rows_out"), NT + 2)
            sp.dma_start(out[0, t * P:(t + 1) * P, :], OROWS[:, t, :]).then_inc(sem("stored"), 16)
        sp.wait_ge(sem("stored"), 16 * TT)

    @block.gpsimd
    def _(pool):
        def low_part(slot, u):
            pool.wait_ge(sem("hi_done"), slot + (u + 1))
            pool.tensor_tensor(WLO[:, u % 2], WRAW[:, u], WHI[:, u % 2].bitcast(F32), ALU.subtract
                               ).then_inc(sem("lo_done"), 1)

        def low_parts(g0, groups):
            with pool.Fori(0, groups) as i:
                for u in range(4):
                    low_part(i * 4 + g0, u)

        low_parts(0, RUN_RWO[0] // 4)
        for u in range(2):
            low_part(RUN_RWO[0], u)
        between_mask = cst("between").unsqueeze(1).to_broadcast([P, NT, P])
        for c in range(NC):
            pool.wait_ge(sem(f"blocks_in{c % 2}"), 32 * (c // 2 + 1))
            if c >= 2:
                pool.wait_ge(sem("dm_mm"), c - 1)
            if c == 0:
                pool.wait_ge(sem("inverse_done"), 1)
            pool.tensor_tensor(BETW[c % 2], TTX[:, c % 2], between_mask, ALU.mult).then_inc(sem("between_done"), 1)
        for u in range(2, 4):
            low_part(RUN_RWO[0], u)
        low_parts(RUN_RWO[0] + 4, (SLOTS - RUN_RWO[0]) // 4 - 1)

    @block.tensor
    def _(pe):
        def split_product(dst, g_slot, block_at, k_act, first, last):
            hi, lo = block_at(WHI[:, g_slot]), block_at(WLO[:, g_slot])
            pe.matmul(dst, hi, ALO[:, k_act, :], start=first, stop=False)
            pe.matmul(dst, hi, AHI[:, k_act, :], start=False, stop=False)
            return pe.matmul(dst, lo, AHI[:, k_act, :], start=False, stop=last)

        def slot(run, trip, u, a0):
            g0, n0 = run
            pe.wait_ge(sem("lo_done"), trip * 4 + (g0 + u + 1))
            pe.wait_ge(sem("bank_free"), trip * 4 + (n0 + u - 3))
            for k in range(NT):
                if u == 0:
                    pe.wait_ge(sem("act_ready"), a0 + k + 1)
                last = split_product(BANK[u], u % 2, lambda w, k=k: w[:, k, :], k, k == 0, k == NT - 1)
            last.then_inc(sem("mm_done"), 1)

        def dense(run, a0, groups=2, after=None):
            with pe.Fori(0, groups) as trip:
                for u in range(4):
                    slot(run, trip, u, a0)
                    if after is not None and u:
                        after(trip, u - 1)
                if after is not None:
                    after(trip, 3)

        def turn_four(dst, parts, rows=P):
            for n, part in enumerate(parts):
                last = pe.transpose(dst[:, n * P:(n + 1) * P], part, IDENT[0:rows, 0:rows])
            return last

        def norm_sum(v):
            pe.wait_ge(sem("acc_done"), NT * (v + 1))
            pe.matmul(BANK[4], ONES, ACC[:, :], start=True, stop=True).then_inc(sem("norm_mm"), 1)

        pe.wait_ge(sem("consts_in"), 16)
        pe.wait_ge(sem("prm_in"), 16 * PRM_DMAS)
        pe.transpose(BANK[0][:, 0:P], PRMROWS[:, 0, :], IDENT)
        rest = PARAM_ROWS - P
        pe.transpose(BANK[0][:, P:P + rest], PRMROWS[0:rest, 1, :], IDENT[0:rest, 0:rest]).then_inc(sem("prm_turned"), 1)
        pe.wait_ge(sem("p_in"), 16)
        for layer in range(2):
            for k in range(2):
                turn_four(BANK[4 + 2 * layer + k], [PROWS[:, layer, t, k * P:(k + 1) * P] for t in range(TT)]
                          ).then_inc(sem("p_turned"), 1)
        pe.wait_ge(sem("x_in"), 16 * TT)
        for j in range(NT):
            if j < 4:
                pe.wait_ge(sem("act_ready"), j + 1)
            else:
                pe.wait_ge(sem("xt_done"), j - 3)
            turn_four(BANK[4 + j % 4], [XROWS[:, t, j * P:(j + 1) * P] for t in range(TT)]).then_inc(sem("x_turned"), 1)
        pe.wait_ge(sem("prm_done"), 1)
        for g in range(4):
            pe.wait_ge(sem("lo_done"), g + 1)
            for m in range(4):
                n = 4 * g + m
                if n >= 4:
                    pe.wait_ge(sem("bank_free"), n - 3)
                for k in range(2):
                    def at_block(w, k=k, m=m):
                        return w.rearrange("p k n -> p (k n)")[:, k * TOK + m * P:k * TOK + (m + 1) * P]
                    last = split_product(BANK[m], g % 2, at_block, 2 * (g // 2) + k, k == 0, k == 1)
                last.then_inc(sem("mm_done"), 1)
            if g == 1:
                norm_sum(0)

        pe.wait_ge(sem("lora_in"), 64)
        for k in range(NT):
            pe.wait_ge(sem("lora_mix"), 2 * k + 1)
            pe.matmul(BANK[5][0:LORA, :], LW1[:, 0, k, :], KT[:, k, :], start=(k == 0), stop=(k == NT - 1)
                      ).then_inc(sem("lora_mm"), 1)
            pe.wait_ge(sem("lora_mix"), 2 * k + 2)
            pe.matmul(BANK[6][0:LORA, :], LW1[:, 1, k, :], KH[:, k, :], start=(k == 0), stop=(k == NT - 1)
                      ).then_inc(sem("lora_mm"), 1)
        pe.wait_ge(sem("lora_act"), 2)
        for j in range(NT):
            if j >= 2:
                pe.wait_ge(sem("sig_done"), 2 * (j - 1))
            pe.matmul(BANK[4 + j % 2], LW2[:, 0, j * P:(j + 1) * P], TMP[0:LORA, 0, :], start=True, stop=True
                      ).then_inc(sem("z_mm"), 1)
            pe.matmul(BANK[6 + j % 2], LW2[:, 1, j * P:(j + 1) * P], TMP[0:LORA, 1, :], start=True, stop=True
                      ).then_inc(sem("z_mm"), 1)

        pe.wait_ge(sem("tables_in"), 32)

        def head_sum(bank, src, j):
            return pe.matmul(bank[0:HEADS, :], HEADOF[:, j, :], src, start=(j == 0), stop=(j == NT - 1))

        for j in range(NT):
            slot(RUN_K, j // 4, j % 4, A_K)
            if j == 0:
                pe.wait_ge(sem("sig_done"), 2 * NT)
            if j:
                pe.wait_ge(sem("kk_squared"), j)
                head_sum(BANK[4], KT[:, j - 1, :], j - 1)
        pe.wait_ge(sem("kk_squared"), NT)
        head_sum(BANK[4], KT[:, NT - 1, :], NT - 1).then_inc(sem("kk_sum"), 1)

        for j in range(NT):
            if j == 0:
                pe.wait_ge(sem("kk_rstd"), 1)
            if j >= 2:
                pe.wait_ge(sem("kk_unit"), j - 1)
            pe.matmul(BANK[5 + j % 2], HEADROWS[:, j, :], RK[:, :], start=True, stop=True).then_inc(sem("kk_bcast"), 1)
            slot(RUN_R, j // 4, j % 4, A_R)
            if j:
                pe.wait_ge(sem("bonus_mul"), j)
                head_sum(BANK[7], SQ[:, (j - 1) % 2, :], j - 1).then_inc(sem("bonus_mm"), 1)
        pe.wait_ge(sem("bonus_mul"), NT)
        head_sum(BANK[7], SQ[:, (NT - 1) % 2, :], NT - 1).then_inc(sem("bonus_mm"), 1)

        for j in range(NT):
            slot(RUN_V, j // 4, j % 4, A_V)
            if j == 0:
                pe.wait_ge(sem("bonus_kept"), 1)
            if j >= 2:
                pe.wait_ge(sem("bonus_v"), j - 1)
            pe.matmul(BANK[5 + j % 2], HEADROWS[:, j, :], RK[:, :], start=True, stop=True).then_inc(sem("bonus_bcast"), 1)
        with pe.Fori(0, NC // 2) as i:
            for b in range(2):
                c = i * 2 + b
                pe.wait_ge(sem(f"a_in{b}"), i * 48 + 48)
                pe.wait_ge(sem("a_masked"), c + 1)
                for j in range(NT):
                    last = pe.matmul(BANK[4 + b][:, j * CH:(j + 1) * CH], NBX[:, b, j, :], KTC[:, b, j, :],
                                     start=True, stop=True)
                last.then_inc(sem("a_mm"), 1)

        dense(RUN_GATE, A_GATE)
        pe.wait_ge(sem("bank_free"), RUN_GATE[1] + NT)

        def turn_diagonal(c):
            pe.wait_ge(sem("diagonal_done"), c + 1)
            if c:
                pe.wait_ge(sem("dturn_kept"), c)
            for g in range(2):
                m = turn_four(BANK[g], [BDIAG[c % 4][:, 4 * g + m4, :] for m4 in range(4)])
            m.then_inc(sem("dturn_mm"), 1)

        def block_product(banks, lhs, rhs, done):
            for j in range(NT):
                m = pe.matmul(BANK[banks + j // 4][:, (j % 4) * P:(j % 4 + 1) * P], lhs[:, j, :], rhs[:, j, :],
                              start=True, stop=True)
            m.then_inc(done, 1)

        turn_diagonal(0)
        for c in range(NC + 1):
            if c + 1 < NC:
                turn_diagonal(c + 1)
            if c < NC:
                pe.wait_ge(sem("between_done"), c + 1)
                pe.wait_ge(sem("dturn_kept"), c + 1)
                if c:
                    pe.wait_ge(sem("dm_kept"), c)
                block_product(2, BETW[c % 2], BDIAGT[c % 2], sem("dm_mm"))
            if c:
                pe.wait_ge(sem("dm_kept"), c)
                if c >= 2:
                    pe.wait_ge(sem("t_kept"), c - 1)
                block_product(4, BPROD[(c - 1) % 2], BDIAG[(c - 1) % 4], sem("t_mm"))

        pe.wait_ge(sem("state_zero"), 1)
        pe.wait_ge(sem("t_kept"), NC)
        with pe.Fori(0, NC // 2) as i:
            for b in range(2):
                c = i * 2 + b
                pe.wait_ge(sem(f"chunk_in{b}"), i * 176 + 176)
                pe.wait_ge(sem("v_kept"), c * 2 + 2)
                pe.wait_ge(sem("w_kept"), c * 2 + 2)
                for j in range(NT):
                    m = pe.matmul(BANK[j // 4][:, (j % 4) * P:(j % 4 + 1) * P], KHX[:, b, j, :],
                                  KRC[:, b, j].rearrange("p n t -> p (n t)"), start=True, stop=True)
                    if j % 4 == 3:
                        m.then_inc(sem("kr_mm"), 1)
                for j in range(NT):
                    m = pe.matmul(BANK[2][:, j * CH:(j + 1) * CH], NBX[:, b, j, :], KRC[:, b, j, 1, :], start=True, stop=True)
                m.then_inc(sem("kr_mm"), 1)
                pe.wait_ge(sem("u_kept"), c * 2 + 2)
                pe.wait_ge(sem("state_done"), c * 2 + 2)
                for n, src in enumerate((KHX, NBX)):
                    for g in range(2):
                        turn_four(BANK[4 + 2 * n + g], [src[:, b, 4 * g + m, :] for m in range(4)]
                                  ).then_inc(sem("rows_mm"), 1)
                pe.wait_ge(sem("y_done"), c + 1)
                turn_four(BANK[3], [VTX[:, b, m, :] for m in range(4)]).then_inc(sem("rows_mm"), 1)
                pe.wait_ge(sem("kr_masked"), c * 5 + 2)
                turn_four(BANK[0], [VTX[:, b, 4 + m, :] for m in range(4)]).then_inc(sem("rows_mm"), 1)
                pe.wait_ge(sem("kr_masked"), c * 5 + 5)
                pe.wait_ge(sem("v_kept"), c * 2 + 4)
                for j in range(NT):
                    o = BANK[1 + j // 4][:, (j % 4) * P:(j % 4 + 1) * P]
                    pe.matmul(o, KTX[:, b, j, :], STX[:, j, :], start=True, stop=False)
                    m = pe.matmul(o, AKX[:, j, :], VX[:, j, :], start=False, stop=True)
                    if j % 4 == 3:
                        m.then_inc(sem("w_mm"), 1)
                for j in range(NT):
                    o = BANK[3][:, j * CH:(j + 1) * CH]
                    pe.matmul(o, STX[:, j, :], KRC[:, b, j, 1, :], start=(j == 0), stop=False, skip_group_check=True)
                    pe.matmul(o, VX[:, j, :], RC[:, j, 0, :], start=False, stop=False, skip_group_check=True)
                pe.wait_ge(sem("rows_kept"), c * 4 + 4)
                for g in range(2):
                    pe.wait_ge(sem("w_kept"), c * 2 + (3 + g))
                    for m4 in range(4):
                        j = 4 * g + m4
                        m = pe.matmul(BANK[4 + g][:, m4 * P:(m4 + 1) * P], TTX[:, b, j, :], WX[:, j, :], start=True, stop=True)
                    m.then_inc(sem("u_mm"), 1)
                for g in range(2):
                    pe.wait_ge(sem("u_kept"), c * 2 + (3 + g))
                    for m4 in range(4):
                        j = 4 * g + m4
                        o = BANK[6 + g][:, m4 * P:(m4 + 1) * P]
                        pe.matmul(o, KS[:, 0, j, :], VX[:, j, :], start=True, stop=False)
                        m = pe.matmul(o, KS[:, 1, j, :], UX[:, j, :], start=False, stop=True)
                    m.then_inc(sem("s_mm"), 1)
                for j in range(NT):
                    m = pe.matmul(BANK[3][:, j * CH:(j + 1) * CH], UX[:, j, :], RC[:, j, 1, :], start=False,
                                  stop=True, skip_group_check=True)
                m.then_inc(sem("y_mm"), 1)

        pe.wait_ge(sem("y_done"), NC + 1)
        pe.wait_ge(sem("state_done"), NC * 2 + 2)
        center = cst("center")
        for j in range(NT):
            if j >= 2:
                pe.wait_ge(sem("gn_squared"), j - 1)
            pe.matmul(BANK[4 + j % 2], center, YT[:, j, :], start=True, stop=True).then_inc(sem("gn_center"), 1)
            if j:
                pe.wait_ge(sem("gn_squared"), j)
                head_sum(BANK[6], SQ[:, (j - 1) % 2, :], j - 1).then_inc(sem("gn_mm"), 1)
        pe.wait_ge(sem("gn_squared"), NT)
        head_sum(BANK[6], SQ[:, (NT - 1) % 2, :], NT - 1).then_inc(sem("gn_mm"), 1)
        pe.wait_ge(sem("gn_in"), 32)
        pe.wait_ge(sem("gn_rstd"), 1)
        for j in range(NT):
            if j >= 2:
                pe.wait_ge(sem("gn_scaled"), j - 1)
            pe.matmul(BANK[4 + j % 2], HEADROWS2[:, j, :], RK2[:, :], start=True, stop=True).then_inc(sem("gn_bcast"), 1)
        dense(RUN_RWO, A_RWO)
        norm_sum(1)
        dense(RUN_PE0, A_PE0)
        norm_sum(2)

        dense(RUN_DQ, A_DA)
        dense(RUN_DK, A_DA)

        def turn_v(trip, u):
            pe.wait_ge(sem("bank_free"), trip * 4 + (RUN_DV[1] + u + 1))
            pe.wait_ge(sem("v_turned"), trip * 4 + (u + 1))
            turn_four(BANK[4 + u % 2], [VSTAGE[:, u % 2, t * P:(t + 1) * P] for t in range(TT)]
                      ).then_inc(sem("v_mm"), 1)

        pe.wait_ge(sem("norm_sqrt"), 3)
        dense(RUN_DV, A_DA, after=turn_v)
        dense(RUN_DG, A_DA)
        pe.wait_ge(sem("v_turned"), NT + 2)
        pe.wait_ge(sem("bank_free"), RUN_DG[1] + NT)
        steps = [(b, q) for b in range(2) for q in range(TT)]
        with pe.Fori(0, NT // 2) as i:
            def scores(s):
                b, q = steps[s]
                if q == 0:
                    pe.wait_ge(sem(f"head_in{b}"), i * 48 + 48)
                pe.wait_ge(sem("exp_done"), i * 16 + (2 * s + 2))
                w = (q + 1) * P
                for comp in range(2):
                    cp = slice(comp * CH, (comp + 1) * CH)
                    m = pe.matmul(PS[:, 2 * (s % 2) + comp, 0:w], QS[cp, b, q * P:(q + 1) * P], KSD[cp, b, 0:w],
                                  start=True, stop=True)
                m.then_inc(sem("score_mm"), 1)

            def turns(s):
                pe.wait_ge(sem("att_done"), i * 8 + (s + 1))
                pe.wait_ge(sem("att_turned"), i * 8 + (s + 1))
                for t in range(steps[s][1] + 1):
                    m = pe.transpose(BANK[4 + s % 2][:, t * P:(t + 1) * P], ATT[:, s % 2, t * P:(t + 1) * P], IDENT)
                m.then_inc(sem("turn_mm"), 1)

            def values(s):
                b, q = steps[s]
                pe.wait_ge(sem("att_turned"), i * 8 + (s + 3))
                if q == 0:
                    pe.wait_ge(sem("head_out"), i * 2 + (b + 1))
                for t in range(q + 1):
                    m = pe.matmul(BANK[6 + b][:, q * P:(q + 1) * P], VS[:, b, t, :], ATTT[:, s % 2, t * P:(t + 1) * P],
                                  start=(t == 0), stop=(t == q))
                m.then_inc(sem("value_mm"), 1)

            scores(0)
            scores(1)
            for s in range(8):
                if s < 6:
                    scores(s + 2)
                if s:
                    values(s - 1)
                turns(s)
            values(7)
        pe.wait_ge(sem("head_out"), NT + 2)
        for j in range(NT):
            pe.wait_ge(sem("sub_squared"), j + 1)
            pe.matmul(BANK[4][0:NT, :], TILEOF[:, j, :], SQ[:, j % 2, :], start=(j == 0), stop=(j == NT - 1)
                      ).then_inc(sem("sub_mm"), 1)
        pe.wait_ge(sem("sub_rstd"), 1)
        for j in range(NT):
            if j >= 2:
                pe.wait_ge(sem("sub_scaled"), j - 1)
            pe.matmul(BANK[5 + j % 2], TILEROWS[:, j, :], RK8[:, :], start=True, stop=True).then_inc(sem("sub_bcast"), 1)
        dense(RUN_DAO, A_DAO)
        norm_sum(3)
        dense(RUN_PE1, A_PE1)
        norm_sum(4)
        norm_sum(5)

        dense(RUN_CC, A_CONV, 8)
        dense(RUN_CO, A_CO)
        norm_sum(6)

        def turn_sv(trip, u):
            pe.wait_ge(sem("bank_free"), RUN_KV[1] + HT4 + u + 1)
            pe.wait_ge(sem("sv_turned"), u + 1)
            turn_four(BANK[4 + u % 2], [SVST[:, u % 2, t * P:(t + 1) * P] for t in range(TT)]).then_inc(sem("sv_mm"), 1)

        for u in range(4):
            slot(RUN_KV, 0, u, A_KV)
        pe.wait_ge(sem("norm_sqrt"), 7)
        for u in range(4):
            slot(RUN_KV, 1, u, A_KV)
            if u:
                turn_sv(1, u - 1)
        turn_sv(1, 3)
        dense(RUN_QG, A_QG)
        pe.wait_ge(sem("sv_turned"), HT4 + 2)
        pe.wait_ge(sem("bank_free"), RUN_QG[1] + NT)
        pair_steps = [(b, q) for b in range(2) for q in range(TT)]
        NS = len(pair_steps)
        with pe.Fori(0, HT4 // 2) as i:
            def logits(s):
                b, q = pair_steps[s]
                if q == 0:
                    pe.wait_ge(sem(f"pair_in{b}"), i * 48 + 48)
                pe.wait_ge(sem("z_free"), i * NS + (s + 1))
                w = (q + 1) * P
                for h in range(2):
                    hp = slice(h * CH, (h + 1) * CH)
                    m = pe.matmul(PS[:, 2 * (s % 2) + h, 0:w], SQH[hp, b, q * P:(q + 1) * P], SKH[hp, b, 0:w],
                                  start=True, stop=True)
                m.then_inc(sem("logit_mm"), 1)

            def turns(s):
                pe.wait_ge(sem("weights_done"), i * NS + (s + 3))
                for h in range(2):
                    pe.wait_ge(sem("weights_turned"), i * 2 * NS + (2 * s + h + 1))
                    for t in range(pair_steps[s][1] + 1):
                        m = pe.transpose(BANK[4 + h][:, t * P:(t + 1) * P], SATT[:, s % 2, h, t * P:(t + 1) * P], IDENT)
                    m.then_inc(sem("wturn_mm"), 1)

            def values(s):
                b, q = pair_steps[s]
                if q == 0:
                    pe.wait_ge(sem("pair_out"), i * 2 + (b + 1))
                for h in range(2):
                    pe.wait_ge(sem("weights_turned"), i * 2 * NS + (2 * s + h + 3))
                    hp = slice(h * CH, (h + 1) * CH)
                    for t in range(q + 1):
                        m = pe.matmul(BANK[6 + b][hp, q * P:(q + 1) * P], SVH[:, b, t, hp],
                                      SATTT[:, s % 2, h, t * P:(t + 1) * P], start=(t == 0), stop=(t == q))
                m.then_inc(sem("pair_mm"), 1)

            logits(0)
            logits(1)
            for s in range(NS):
                if s < NS - 2:
                    logits(s + 2)
                if s:
                    values(s - 1)
                turns(s)
            values(NS - 1)
        g0, n0 = RUN_BO
        for u in range(4):
            pe.wait_ge(sem("lo_done"), g0 + u + 1)
            for m2 in range(2):
                n = n0 + 2 * u + m2
                pe.wait_ge(sem("bank_free"), n - 3)
                for k in range(HT4):
                    if u == 0:
                        pe.wait_ge(sem("act_ready"), A_BO + k + 1)

                    def at_block(w, k=k, m2=m2):
                        c = k * 2 * P + m2 * P
                        return w.rearrange("p k n -> p (k n)")[:, c:c + P]
                    last = split_product(BANK[(2 * u + m2) % 4], u % 2, at_block, k, k == 0, k == HT4 - 1)
                last.then_inc(sem("mm_done"), 1)
        norm_sum(7)
        pe.wait_ge(sem("norm_sqrt"), 8)
        for j in range(NT):
            pe.wait_ge(sem("final_scaled"), j + 1)
            pe.wait_ge(sem("rows_out"), j + 1)
            turn_four(BANK[4 + j % 2], [FT[:, j % 2, t * P:(t + 1) * P] for t in range(TT)]).then_inc(sem("final_mm"), 1)

    @block.scalar
    def _(act):
        def hi(g, trip=0):
            act.wait_ge(sem(f"w_landed{g % 4}"), trip * 16 + 16 * (g // 4 + 1))
            if g >= 2:
                act.wait_ge(sem("mm_done"), trip * 4 + outs_after(g - 2))
            act.activation(WHI[:, g % 2], WRAW[:, g % 4], ACT.Copy).then_inc(sem("hi_done"), 1)

        def run(r, body=None, groups=2, body_end=None):
            with act.Fori(0, groups) as trip:
                for u in range(4):
                    hi(r[0] + u + 2, trip)
                    if body is not None:
                        body(trip, u)
                if body_end is not None:
                    body_end(trip)

        def split_plain(src, a0, ready, r0, tiles=NT, before=0):
            if before:
                act.wait_ge(sem("mm_done"), before)
            for k in range(tiles):
                act.wait_ge(ready, r0 + k + 1)
                act.activation(AHI[:, k, :], src(k), ACT.Copy).then_inc(sem("hi_act"), 1)

        def split_scaled(g, before):
            act.wait_ge(sem("mm_done"), before)
            for k in range(NT):
                act.activation(AHI[:, k, :], XT[:, k, :], ACT.Identity, scale=prm(g, k)).then_inc(sem("hi_act"), 1)

        def square(v, j, u):
            act.wait_ge(sem("xt_done"), j + (NT * v + 1))
            if v or j >= 2:
                act.wait_ge(sem("acc_done"), j + (NT * v - 1))
            act.activation(SQ[:, u % 2, :], row(XT, j), ACT.Square).then_inc(sem("sq_done"), 1)

        def root(v):
            act.wait_ge(sem("norm_mm"), v + 1)
            act.activation(RB[:, :], BANK[4], ACT.Sqrt, bias=eps(0), scale=1.0 / DM).then_inc(sem("norm_sqrt"), 1)

        def rows_in(g, src, n):
            t, r = divmod(g * NT, P)
            act.dma_start(PRMROWS[r:r + n, t, :], src).then_inc(sem("prm_in"), 16)

        for g, name in ((G_RW, "rw_norm"), (W0, "rw_w0"), (A0, "rw_a0"), (K_K, "rw_k_k"), (K_A, "rw_k_a"),
                        (LN_W, "rw_ln_w"), (LN_B, "rw_ln_b"), (G_DA, "da_norm"), (G_CONV, "norm_a_2"), (G_B, "norm_b_2")):
            rows_in(g, a[name].rearrange("a (j p) -> (a j) p", p=P), NT)
        rows_in(MU_R, a["rw_mu"][0].rearrange("m (j p) -> (m j) p", p=P), 6 * NT)
        rows_in(R_K, a["rw_r_k"][0].rearrange("(j h) d -> j (h d)", h=2), NT)
        for g, n in ((G_PE0, 0), (G_PE1, 1)):
            rows_in(g, a["pe_norm"][n:n + 1].rearrange("a (j p) -> (a j) p", p=P), NT)
        for g, name in ((G_FIRST, "final_norm"), (G_KV, "norm_kv_2"), (G_LAST, "norm_f_2")):
            rows_in(g, a[name].rearrange("(j p) -> j p", p=P), NT)
        rows_in(CONV0, a["conv_a_2"][0].rearrange("m (j p) -> (m j) p", p=P), 3 * NT)
        rows_in(SUBLN, a["da_subln"], 1)
        hi(0)
        hi(1)
        for t in range(4):
            act.wait_ge(sem("p_turned"), t + 1)
            act.activation(AHI[:, t, :], BANK[4 + t], ACT.Copy).then_inc(sem("hi_act"), 1)
        for j in range(NT):
            square(0, j, j)
        for g in range(4):
            hi(g + 2)
            if g == 1:
                root(0)
            for n in range(4 * g, 4 * g + 4):
                act.wait_ge(sem("bank_free"), n + 1)
                act.dma_start(D_PLE[g // 2, (g % 2) * 4 + n % 4], PLEOUT[:, n % 4, :]).then_inc(sem(f"ple_out{n % 4}"), 16)

        act.wait_ge(sem("lora_mm"), 2 * NT)
        act.activation(TMP[0:LORA, 0, :], BANK[5][0:LORA, :], ACT.Tanh).then_inc(sem("lora_act"), 1)
        act.activation(TMP[0:LORA, 1, :], BANK[6][0:LORA, :], ACT.Copy).then_inc(sem("lora_act"), 1)
        for j in range(NT):
            act.wait_ge(sem("z_mm"), 2 * j + 1)
            if j >= 2:
                act.wait_ge(sem("scan_done"), j - 1)
            act.activation(TMP[:, 2 + j % 2, :], BANK[4 + j % 2], ACT.Sigmoid, bias=prm(W0, j)).then_inc(sem("sig_done"), 1)
            act.wait_ge(sem("z_mm"), 2 * j + 2)
            act.activation(NB[:, j, :], BANK[6 + j % 2], ACT.Sigmoid, bias=prm(A0, j)).then_inc(sem("sig_done"), 1)

        def mixed(k):
            return SQ[:, k % 2, :]

        split_plain(mixed, A_K, sem("mix_done"), 0)
        for j in range(NT):
            hi(RUN_K[0] + j + 2)
            act.wait_ge(sem("bank_free"), RUN_K[1] + j + 1)
            act.activation(KT[:, j, :], KH[:, j, :], ACT.Square, scale=prm(K_K, j)).then_inc(sem("kk_squared"), 1)
        act.wait_ge(sem("kk_sum"), 1)
        act.activation(RK[:, :], BANK[4][0:HEADS, :], ACT.Sqrt).then_inc(sem("kk_sqrt"), 1)
        def spill(j):
            for src, dst in ((KT, D_KT), (RT, D_RT), (KH, D_KH), (NB, D_NB)):
                act.dma_start(dst.rearrange("c p j t -> p j c t")[:, j], src[:, j, :].rearrange("p (c t) -> p c t", t=CH)
                              ).then_inc(sem("spilled"), 16)

        split_plain(mixed, A_R, sem("mix_done"), NT, before=RUN_R[1])
        for j in range(NT):
            if j:
                act.wait_ge(sem("bonus_mul"), j)
                spill(j - 1)
            act.activation(TMP[:, 0, :], RT[:, j, :], ACT.Exp, scale=-DECAY).then_inc(sem("decays"), 1)
            act.activation(TMP[:, 1, :], RT[:, j, :], ACT.Exp, scale=DECAY).then_inc(sem("decays"), 1)
            hi(RUN_R[0] + j + 2)
        act.wait_ge(sem("bonus_mul"), NT)
        spill(NT - 1)
        split_plain(mixed, A_V, sem("mix_done"), 2 * NT, before=RUN_V[1])
        v_to = D_VT.rearrange("c p j t -> p j c t")
        for j in range(NT):
            hi(RUN_V[0] + j + 2)
            act.wait_ge(sem("bonus_v"), j + 1)
            act.dma_start(v_to[:, j], TMP[:, j % 2, :].rearrange("p (c t) -> p c t", t=CH)).then_inc(sem(f"v_out{j % 2}"), 16)
            act.dma_start(D_BV[j], TMP[:, 2 + j % 2, :]).then_inc(sem(f"v_out{j % 2}"), 16)
        with act.Fori(0, NC // 2) as i:
            for b in range(2):
                c = i * 2 + b
                act.wait_ge(sem("a_masked"), c + 3)
                for h in range(2):
                    act.dma_start(D_A[bass.ds(c, 1), :, h].rearrange("c j s t -> s (c j) t"),
                                  NA[h * CH:(h + 1) * CH, b]).then_inc(sem(f"a_out{b}"), 16)
        split_plain(mixed, A_GATE, sem("mix_done"), 3 * NT, before=RUN_GATE[1])
        act.wait_ge(sem("bank_free"), RUN_GATE[1])

        def gate_body(trip, u):
            act.wait_ge(sem("mm_done"), trip * 4 + (RUN_GATE[1] + u + 1))
            act.activation(row(GT, trip * 4 + u), BANK[u], ACT.Silu).then_inc(sem("bank_free"), 1)

        run(RUN_GATE, gate_body)
        for c in range(NC + 1):
            if c < NC:
                act.wait_ge(sem("dturn_mm"), c + 1)
                if c >= 2:
                    act.wait_ge(sem("dm_mm"), c - 1)
                act.activation(BDIAGT[c % 2], PS[:, 0:2, :].rearrange("p g (j t) -> p (g j) t", t=P), ACT.Copy
                               ).then_inc(sem("dturn_kept"), 1)
            if c:
                act.wait_ge(sem("t_mm"), c)
                act.activation(TALL[:, c - 1], PS[:, 4:6, :].rearrange("p g (j t) -> p (g j) t", t=P), ACT.Copy
                               ).then_inc(sem("t_kept"), 1)
        with act.Fori(0, NC // 2) as i:
            for b in range(2):
                c = i * 2 + b
                for n in range(4):
                    act.wait_ge(sem("rows_mm"), c * 6 + (n + 1))
                    g = n % 2
                    act.activation(KS[:, n // 2, 4 * g:4 * g + 4, :], BANK[4 + n], ACT.Copy).then_inc(sem("rows_kept"), 1)
                for g in range(2):
                    act.wait_ge(sem("rows_mm"), c * 6 + (5 + g))
                    act.activation(VX[:, 4 * g:4 * g + 4, :], BANK[3 - 3 * g], ACT.Copy).then_inc(sem("v_kept"), 1)
                for g in range(2):
                    act.wait_ge(sem("w_mm"), c * 2 + (g + 1))
                    act.activation(WX[:, 4 * g:4 * g + 4, :], BANK[1 + g], ACT.Copy).then_inc(sem("w_kept"), 1)
                for g in range(2):
                    act.wait_ge(sem("u_mm"), c * 2 + (g + 1))
                    act.activation(UX[:, 4 * g:4 * g + 4, :], BANK[4 + g], ACT.Copy).then_inc(sem("u_kept"), 1)
        for j in range(NT):
            act.wait_ge(sem("gn_center"), j + 1)
            act.activation(YT[:, j, :], BANK[4 + j % 2], ACT.Copy).then_inc(sem("gn_kept"), 1)
            if j >= 2:
                act.wait_ge(sem("gn_mm"), j - 1)
            act.activation(SQ[:, j % 2, :], BANK[4 + j % 2], ACT.Square).then_inc(sem("gn_squared"), 1)
        act.wait_ge(sem("gn_mm"), NT)
        act.activation(RK2[:, :], BANK[6][0:HEADS, :], ACT.Sqrt, bias=eps(1)[0:HEADS], scale=1.0 / CH
                       ).then_inc(sem("gn_sqrt"), 1)
        split_plain(lambda k: YT[:, k, :], A_RWO, sem("gn_done"), 0)

        def residual(v):
            return lambda trip, u: square(v, trip * 4 + u, u)

        run(RUN_RWO, residual(1))
        split_scaled(G_PE0, RUN_PE0[1])
        root(1)

        def embed(v, n):
            def body(trip, u):
                act.wait_ge(sem("bank_free"), trip * 4 + (n + u + 1))
                act.activation(PTMP[:, u % 2, :], PTMP[:, u % 2, :], ACT.Sigmoid).then_inc(sem("ple_gate"), 1)
                square(v, trip * 4 + u, u)
            return body

        run(RUN_PE0, embed(2, RUN_PE0[1]))
        split_scaled(G_DA, RUN_DQ[1])
        root(2)
        act.wait_ge(sem("lambda_sums"), 2)
        act.activation(STAT[:, 2, 2:4], STAT[:, 2, 0:2], ACT.Exp).then_inc(sem("lambda_exp"), 1)
        for r, k0 in ((RUN_DQ, 0), (RUN_DK, NT)):
            def rotate(trip, u, r=r, k0=k0):
                act.wait_ge(sem("rope_done"), trip * 4 + (k0 + u + 1))
                for q in range(4):
                    m = act.activation(RTMP[32 * (q ^ 1):32 * (q ^ 1) + 32, 0, :], BANK[u][32 * q:32 * q + 32, :], ACT.Copy)
                m.then_inc(sem("rotated"), 1)
            run(r, rotate)

        def keep_v(trip, u):
            act.wait_ge(sem("v_mm"), trip * 4 + (u + 1))
            j = trip * 4 + u
            act.activation(DV[:, :, bass.ds(j * P, P)], BANK[4 + u % 2].rearrange("p (t d) -> p t d", t=TT), ACT.Copy
                           ).then_inc(sem("v_turned"), 1)

        run(RUN_DV, lambda trip, u: keep_v(trip, u - 1) if u else None, body_end=lambda trip: keep_v(trip, 3))

        def d_gate(trip, u):
            act.wait_ge(sem("bank_free"), trip * 4 + (RUN_DG[1] + u + 1))
            j = trip * 4 + u
            act.activation(row(DGT, j), row(DGT, j), ACT.Silu).then_inc(sem("dg_done"), 1)

        run(RUN_DG, d_gate)
        with act.Fori(0, NT // 2) as i:
            def exps(s):
                w = (s % TT + 1) * P
                act.wait_ge(sem("neg_max"), i * 8 + (s + 1))
                for comp in range(2):
                    act.activation(ES[:, s % 2, comp, 0:w], PS[:, 2 * (s % 2) + comp, 0:w], ACT.Exp,
                                   bias=STAT[:, s % 2, 2 + comp:3 + comp], scale=QK_SCALE,
                                   accum_out=STAT[:, s % 2, 4 + comp:5 + comp]).then_inc(sem("exp_done"), 1)

            def keep_att(s):
                w = (s % TT + 1) * P
                act.wait_ge(sem("turn_mm"), i * 8 + (s + 3))
                act.wait_ge(sem("value_mm"), i * 8 + (s + 7))
                act.activation(ATTT[:, s % 2, 0:w], BANK[4 + s % 2][:, 0:w], ACT.Copy).then_inc(sem("att_turned"), 1)

            exps(0)
            for s in range(8):
                if s:
                    keep_att(s - 1)
                if s < 7:
                    exps(s + 1)
            keep_att(7)
        for j in range(NT):
            act.wait_ge(sem("head_out"), j + 3)
            if j >= 2:
                act.wait_ge(sem("sub_mm"), j - 1)
            act.activation(SQ[:, j % 2, :], DQT[:, j, :], ACT.Square).then_inc(sem("sub_squared"), 1)
        act.wait_ge(sem("sub_mm"), NT)
        act.activation(RK8[:, :], BANK[4][0:NT, :], ACT.Sqrt, bias=eps(2)[0:NT], scale=1.0 / P).then_inc(sem("sub_sqrt"), 1)
        split_plain(lambda k: DQT[:, k, :], A_DAO, sem("sub_done"), 0)
        run(RUN_DAO, residual(3))
        split_scaled(G_PE1, RUN_PE1[1])
        root(3)
        run(RUN_PE1, embed(4, RUN_PE1[1]))
        root(4)
        for j in range(NT):
            square(5, j, j)
        split_scaled(G_CONV, RUN_CC[1])
        root(5)
        run(RUN_CC, None, 6)

        def c_gate(trip, u):
            act.wait_ge(sem("bank_free"), trip * 4 + (RUN_CG[1] + u + 1))
            act.activation(CTMP[:, 2 + u % 2, :], CTMP[:, 2 + u % 2, :], ACT.Silu).then_inc(sem("cg_done"), 1)

        run(RUN_CG, c_gate)
        split_plain(lambda k: CV[:, k, :], A_CO, sem("conv_done"), 0, before=RUN_CO[1])
        run(RUN_CO, residual(6))
        split_scaled(G_KV, RUN_KV[1])
        root(6)

        def keep_sv(u):
            act.wait_ge(sem("sv_mm"), u + 1)
            act.activation(SV[:, :, u * P:(u + 1) * P], BANK[4 + u % 2].rearrange("p (t d) -> p t d", t=TT), ACT.Copy
                           ).then_inc(sem("sv_turned"), 1)

        for u in range(NT):
            hi(RUN_KV[0] + u + 2)
            if u > HT4:
                keep_sv(u - HT4 - 1)
        keep_sv(HT4 - 1)
        split_scaled(G_B, RUN_QG[1])
        for u in range(NT):
            hi(RUN_QG[0] + u + 2)
            if u >= HT4:
                act.wait_ge(sem("bank_free"), RUN_QG[1] + u + 1)
                act.activation(SGT[:, u - HT4, :], SGT[:, u - HT4, :], ACT.Silu).then_inc(sem("sg_done"), 1)
        NS = 2 * TT
        own = Clock(act, sem("act_chain"))
        with act.Fori(0, HT4 // 2) as i:
            own.enter(i, 2 * NS)
            act.preload_act_table_set("natural_log_exp_and_others")

            def softplus_parts(s):
                w = (s % TT + 1) * P
                act.wait_ge(sem("logit_mm"), i * NS + (s + 1))
                act.wait_ge(sem("sp_done"), i * NS + (s + 1))
                z = SAB[:, s % 2, :, 0:w]
                own.step(act.activation(z, PS[:, 2 * (s % 2):2 * (s % 2) + 2, 0:w], ACT.Abs))
                own.step(act.activation(z, z, ACT.Exp, scale=-1.0))
                act.activation(z, z, ACT.Ln, bias=eps(3)).then_inc(sem("ln_done"), 1)

            def weights_of(s):
                w = (s % TT + 1) * P
                act.wait_ge(sem("log_weights"), i * NS + (s + 1))
                act.wait_ge(sem("wturn_mm"), i * 2 * NS + (2 * s + 2))
                act.activation(SATT[:, s % 2, :, 0:w], SSUF[:, s % 2, :, 0:w], ACT.Exp).then_inc(sem("weights_done"), 1)

            softplus_parts(0)
            for s in range(NS):
                if s < NS - 1:
                    softplus_parts(s + 1)
                weights_of(s)
            own.leave(HT4 // 2)
        split_plain(lambda k: SQT[:, k, :], A_BO, sem("pair_out"), 2, HT4, before=RUN_BO[1])
        for u in range(4):
            if u < 2:
                hi(RUN_BO[0] + u + 2)
            for j in range(2 * u, 2 * u + 2):
                square(7, j, j)
        root(7)
        for j in range(NT):
            act.wait_ge(sem("final_mm"), j + 1)
            act.activation(OROWS[:, :, j * P:(j + 1) * P], BANK[4 + j % 2].rearrange("p (t d) -> p t d", t=TT), ACT.Copy
                           ).then_inc(sem("rows_out"), 1)

    @block.vector
    def _(dve):
        for name, n in (("a_mm", 2), ("a_masked", 2), ("y_mm", 2), ("v_kept", 2), ("w_kept", 2), ("u_kept", 2),
                        ("state_done", 2), ("y_done", 1), ("v_turned", 2), ("exp_done", 4), ("turn_mm", 2),
                        ("att_turned", 2), ("value_mm", 2 * TT), ("head_out", 2), ("rope_done", 1), ("sv_turned", 2),
                        ("z_free", 2), ("sp_done", 2), ("wturn_mm", 4), ("weights_turned", 2), ("pair_mm", 2 * TT),
                        ("pair_out", 2), ("rows_out", 2), ("weights_done", 2), ("a_out0", 32), ("a_out1", 32)):
            dve.sem_inc(sem(name), n)
        own = Clock(dve, sem("dve_chain"))
        tt, ts, stt = dve.tensor_tensor, dve.tensor_scalar, dve.scalar_tensor_tensor

        def got(n, trip=0):
            dve.wait_ge(sem("mm_done"), trip * 4 + (n + 1))

        def lo_plain(src, a0, tiles=NT):
            for k in range(tiles):
                dve.wait_ge(sem("hi_act"), a0 + k + 1)
                tt(ALO[:, k, :], src(k), AHI[:, k, :].bitcast(F32), ALU.subtract).then_inc(sem("act_ready"), 1)

        def lo_scaled(g, a0):
            for k in range(NT):
                dve.wait_ge(sem("hi_act"), a0 + k + 1)
                stt(out=ALO[:, k, :], in0=XT[:, k, :], scalar=prm(g, k), in1=AHI[:, k, :].bitcast(F32),
                    op0=ALU.mult, op1=ALU.subtract).then_inc(sem("act_ready"), 1)

        def accumulate(v, j, u):
            dve.wait_ge(sem("sq_done"), j + (NT * v + 1))
            sq = SQ[:, u % 2, :]
            if isinstance(j, int) and j == 0:
                dve.tensor_copy(ACC[:, :], sq).then_inc(sem("acc_done"), 1)
            else:
                dve.wait_ge(sem("acc_done"), j + NT * v)
                tt(ACC[:, :], ACC[:, :], sq, ALU.add).then_inc(sem("acc_done"), 1)

        def rstd(v):
            dve.wait_ge(sem("norm_sqrt"), v + 1)
            own.step(dve.reciprocal(RB[:, :], RB[:, :]))

        def mix(mu, a0, m0):
            def one(k):
                if k >= 2:
                    dve.wait_ge(sem("act_ready"), a0 + k - 1)
                stt(out=SQ[:, k % 2, :], in0=DX[:, k, :], scalar=prm(mu, k), in1=H[:, k, 1:TOK + 1],
                    op0=ALU.mult, op1=ALU.add).then_inc(sem("mix_done"), 1)
            one(0)
            for k in range(NT):
                if k + 1 < NT:
                    one(k + 1)
                dve.wait_ge(sem("hi_act"), a0 + k + 1)
                tt(ALO[:, k, :], SQ[:, k % 2, :], AHI[:, k, :].bitcast(F32), ALU.subtract).then_inc(sem("act_ready"), 1)

        dve.wait_ge(sem("prm_turned"), 1)
        own.step(dve.tensor_copy(PRM[:, 0:PARAM_ROWS], BANK[0][:, 0:PARAM_ROWS]))
        dve.memset(PRM[:, PARAM_ROWS:PARAM_ROWS + 1], 0.0).then_inc(sem("prm_done"), 1)
        for t in range(4):
            dve.wait_ge(sem("hi_act"), t + 1)
            tt(ALO[:, t, :], BANK[4 + t], AHI[:, t, :].bitcast(F32), ALU.subtract).then_inc(sem("act_ready"), 1)
        for j in range(NT):
            dve.wait_ge(sem("x_turned"), j + 1)
            dve.tensor_copy(XT[:, j, :], BANK[4 + j % 4]).then_inc(sem("xt_done"), 1)
            if j:
                accumulate(0, j - 1, j - 1)
        accumulate(0, NT - 1, NT - 1)

        def embed_out(n):
            got(n)
            if n >= 4:
                dve.wait_ge(sem(f"ple_out{n % 4}"), 16 * (n // 4))
            dve.tensor_copy(PLEOUT[:, n % 4, :], BANK[n % 4]).then_inc(sem("bank_free"), 1)

        for n in range(8):
            embed_out(n)
        rstd(0)
        own.step(dve.memset(H[:, :, 0:1], 0.0))
        for j in range(NT):
            own.step(stt(out=H[:, j, 1:TOK + 1], in0=XT[:, j, :], scalar=prm(G_RW, j), in1=RB[:, :],
                         op0=ALU.mult, op1=ALU.mult))
            own.step(tt(DX[:, j, :], H[:, j, 0:TOK], H[:, j, 1:TOK + 1], ALU.subtract))
            for mu, dst in ((MU_W, KT), (MU_A, KH)):
                stt(out=dst[:, j, :], in0=DX[:, j, :], scalar=prm(mu, j), in1=H[:, j, 1:TOK + 1],
                    op0=ALU.mult, op1=ALU.add).then_inc(sem("lora_mix"), 1)
            embed_out(8 + j)
        dve.wait_ge(sem("tables_in"), 32)
        for n in range(4):
            dve.wait_ge(sem(f"ple_out{n}"), 64)
        for j in range(NT):
            dve.wait_ge(sem("sig_done"), 2 * j + 1)
            dve.tensor_tensor_scan(RT[:, j, :], KEEP[:, :], TMP[:, 2 + j % 2, :], 0.0, ALU.mult, ALU.add
                                   ).then_inc(sem("scan_done"), 1)
        mix(MU_K, A_K, 0)
        for j in range(NT):
            got(RUN_K[1] + j)
            dve.tensor_copy(KH[:, j, :], BANK[j % 4]).then_inc(sem("bank_free"), 1)
        mix(MU_R, A_R, NT)
        dve.wait_ge(sem("kk_sqrt"), 1)
        own.step(ts(RK[:, :], RK[:, :], 1e-12, None, ALU.max))
        dve.reciprocal(RK[:, :], RK[:, :]).then_inc(sem("kk_rstd"), 1)
        own.step(ts(STAT_KA, PRM[:, K_A * NT:(K_A + 1) * NT], -1.0, 1.0, ALU.mult, ALU.add))
        E, PI, T1, T2, T3 = TMP[:, 0, :], TMP[:, 1, :], TMP[:, 2, :], TMP[:, 3, :], ACC[:, :]

        def chunks(x):
            return x.rearrange("p (c t) -> p c t", t=CH)

        for j in range(NT):
            dve.wait_ge(sem("kk_bcast"), j + 1)
            dve.wait_ge(sem("decays"), 2 * j + 2)
            stt(out=T1, in0=KH[:, j, :], scalar=prm(K_K, j), in1=BANK[5 + j % 2], op0=ALU.mult, op1=ALU.mult
                ).then_inc(sem("kk_unit"), 1)
            ts(T3, NB[:, j, :], prm(K_A, j), STAT_KA[:, j:j + 1], ALU.mult, ALU.add)
            dve.tensor_copy(PC[:, :, j], chunks(E)[:, :, CH - 1])
            dve.wait_ge(sem("kk_unit"), j + 1)
            tt(chunks(KT[:, j, :])[:, :, 1:CH], chunks(T1)[:, :, 1:CH], chunks(E)[:, :, 0:CH - 1], ALU.mult)
            dve.tensor_copy(chunks(KT[:, j, :])[:, :, 0:1], chunks(T1)[:, :, 0:1])
            own.step(stt(out=T2, in0=T1, scalar=-1.0, in1=NB[:, j, :], op0=ALU.mult, op1=ALU.mult))
            own.step(tt(T3, T3, KH[:, j, :], ALU.mult))
            tt(NB[:, j, :], T2, PI, ALU.mult)
            own.step(tt(KH[:, j, :], T3, PI, ALU.mult))
            got(RUN_R[1] + j)
            own.step(tt(RT[:, j, :], BANK[j % 4], E, ALU.mult))
            dve.sem_inc(sem("bank_free"), 1)
            if j >= 2:
                dve.wait_ge(sem("bonus_mm"), j - 1)
            stt(out=SQ[:, j % 2, :], in0=RT[:, j, :], scalar=prm(R_K, j), in1=KH[:, j, :], op0=ALU.mult, op1=ALU.mult
                ).then_inc(sem("bonus_mul"), 1)
        dve.wait_ge(sem("bonus_mm"), NT)
        dve.tensor_copy(RK[:, :], BANK[7][0:HEADS, :]).then_inc(sem("bonus_kept"), 1)
        mix(MU_V, A_V, 2 * NT)
        for j in range(NT):
            got(RUN_V[1] + j)
            if j >= 2:
                dve.wait_ge(sem(f"v_out{j % 2}"), 32 * (j // 2))
            dve.tensor_copy(TMP[:, j % 2, :], BANK[j % 4]).then_inc(sem("bank_free"), 1)
            dve.wait_ge(sem("bonus_bcast"), j + 1)
            dve.wait_ge(sem("bank_free"), RUN_V[1] + j + 1)
            tt(TMP[:, 2 + j % 2, :], TMP[:, j % 2, :], BANK[5 + j % 2], ALU.mult).then_inc(sem("bonus_v"), 1)
        dve.wait_ge(sem("spilled"), 16 * 4 * NC)
        for b in range(2):
            dve.wait_ge(sem(f"v_out{b}"), 128)
        dve.memset(NBX[:, :, :, :], 0.0).then_inc(sem("zeroed"), 1)
        strict_s = cst("strict_s").unsqueeze(1).to_broadcast([P, NT, CH])
        with dve.Fori(0, NC // 2) as i:
            for b in range(2):
                c = i * 2 + b
                dve.wait_ge(sem("a_mm"), c + 3)
                dve.wait_ge(sem(f"a_out{b}"), i * 32 + 32)
                tt(NA[:, b], BANK[4 + b].rearrange("p (j t) -> p j t", t=CH), strict_s, ALU.mult
                   ).then_inc(sem("a_masked"), 1)
        mix(MU_G, A_GATE, 3 * NT)
        for t in (TTX, KTX, KHX):
            dve.memset(t[:, :, :, :], 0.0).then_inc(sem("zeroed"), 1)
        dve.wait_ge(sem("prob_in"), 16)
        blocks = PROB[:, :, :].rearrange("p (b s) (c t) -> p b c s t", b=2, c=2)
        for s in range(1, BL - 1):
            n = BL - 1 - s
            outer = OUTER[:, :, 0:s * n].rearrange("p b (j t) -> p b j t", t=n)
            products = [tt(outer[:, b], blocks[:, b, b, 0:s, s:s + 1].to_broadcast([P, s, n]),
                           blocks[:, b, b, s:s + 1, s + 1:BL].to_broadcast([P, s, n]), ALU.mult) for b in range(2)]
            own.step(products[-1])
            sums = [tt(blocks[:, b, b, 0:s, s + 1:BL], blocks[:, b, b, 0:s, s + 1:BL], outer[:, b], ALU.add)
                    for b in range(2)]
            own.step(sums[-1])
        diagonal = PROB[:, :, :].rearrange("p s t -> p (s t)")[:, 0:CH * CH:CH + 1]
        dve.memset(diagonal, 1.0).then_inc(sem("inverse_done"), 1)
        dve.memset(STX[:, :, :], 0.0).then_inc(sem("state_zero"), 1)
        dve.wait_ge(sem("t_out"), 16)
        dve.memset(VTX[:, :, :, :], 0.0).then_inc(sem("zeroed"), 1)
        diagonal_mask = cst("diagonal").unsqueeze(1).to_broadcast([P, NT, P])

        def diagonal_blocks(c):
            dve.wait_ge(sem(f"blocks_in{c % 2}"), 32 * (c // 2 + 1))
            if c >= 4:
                dve.wait_ge(sem("t_mm"), c - 3)
            tt(BDIAG[c % 4], TTX[:, c % 2], diagonal_mask, ALU.mult).then_inc(sem("diagonal_done"), 1)

        diagonal_blocks(0)
        for c in range(NC):
            if c + 1 < NC:
                diagonal_blocks(c + 1)
            dve.wait_ge(sem("dm_mm"), c + 1)
            if c >= 2:
                dve.wait_ge(sem("t_mm"), c - 1)
            tt(BPROD[c % 2], PS[:, 2:4, :].rearrange("p g (j t) -> p (g j) t", t=P),
               IDENT.unsqueeze(1).to_broadcast([P, NT, P]), ALU.add).then_inc(sem("dm_kept"), 1)
        strict_x = cst("strict_x").rearrange("p (h t) -> p h t", t=CH)
        incl = cst("incl_s")
        with dve.Fori(0, NC // 2) as i:
            for b in range(2):
                c = i * 2 + b
                for g in range(2):
                    dve.wait_ge(sem("kr_mm"), c * 3 + (g + 1))
                    kr = BANK[g].rearrange("p (j n t) -> p j n t", n=2, t=CH)
                    for h in range(2):
                        m = tt(AKX[:, 4 * g:4 * g + 4, h * CH:(h + 1) * CH], kr[:, :, 0, :],
                               strict_x[:, h:h + 1, :].to_broadcast([P, 4, CH]), ALU.mult)
                    m.then_inc(sem("kr_masked"), 1)
                    tt(RC[:, 4 * g:4 * g + 4, 0, :], kr[:, :, 1, :], incl.unsqueeze(1).to_broadcast([P, 4, CH]), ALU.mult
                       ).then_inc(sem("kr_masked"), 1)
                dve.wait_ge(sem("kr_mm"), c * 3 + 3)
                tt(RC[:, :, 1, :], BANK[2].rearrange("p (j t) -> p j t", t=CH),
                   incl.unsqueeze(1).to_broadcast([P, NT, CH]), ALU.mult).then_inc(sem("kr_masked"), 1)
                for g in range(2):
                    st = STX[:, 4 * g:4 * g + 4, :]
                    dve.wait_ge(sem("s_mm"), c * 2 + (g + 1))
                    tt(st, st, BANK[6 + g].rearrange("p (j t) -> p j t", t=P), ALU.add).then_inc(sem("state_sum"), 1)
                    dve.wait_ge(sem("state_sum"), c * 2 + (g + 1))
                    decay = PC[:, bass.ds(c, 1), 4 * g:4 * g + 4].rearrange("p c j -> p (c j)").unsqueeze(2)
                    tt(st, st, decay.to_broadcast([P, 4, P]), ALU.mult).then_inc(sem("state_done"), 1)
                dve.wait_ge(sem("y_mm"), c + 3)
                dve.tensor_copy(YT[:, :, bass.ds(c * CH, CH)], BANK[3].rearrange("p (j t) -> p j t", t=CH)
                                ).then_inc(sem("y_done"), 1)
        dve.wait_ge(sem("gn_sqrt"), 1)
        dve.reciprocal(RK2[:, :], RK2[:, :]).then_inc(sem("gn_rstd"), 1)
        dve.wait_ge(sem("gn_in"), 32)
        for j in range(NT):
            dve.wait_ge(sem("gn_kept"), j + 1)
            dve.wait_ge(sem("gn_bcast"), j + 1)
            y = YTMP[:, j % 2, :]
            stt(out=y, in0=YT[:, j, :], scalar=prm(LN_W, j), in1=BANK[4 + j % 2], op0=ALU.mult, op1=ALU.mult
                ).then_inc(sem("gn_scaled"), 1)
            dve.wait_ge(sem("gn_scaled"), j + 1)
            own.step(stt(out=y, in0=y, scalar=prm(LN_B, j), in1=BVT[:, j, :], op0=ALU.add, op1=ALU.add))
            tt(YT[:, j, :], y, GT[:, j, :], ALU.mult).then_inc(sem("gn_done"), 1)
        lo_plain(lambda k: YT[:, k, :], A_RWO)

        def residual(run, v):
            with dve.Fori(0, 2) as trip:
                for u in range(4):
                    j = trip * 4 + u
                    got(run[1] + u, trip)
                    tt(row(XT, j), row(XT, j), BANK[u], ALU.add).then_inc(sem("xt_done"), 1)
                    dve.wait_ge(sem("xt_done"), j + (NT * v + 1))
                    dve.sem_inc(sem("bank_free"), 1)
                    sum_tile(v, trip, u)

        def sum_tile(v, trip, u):
            j = trip * 4 + u
            dve.wait_ge(sem("sq_done"), j + (NT * v + 1))
            dve.wait_ge(sem("acc_done"), j + NT * v)
            tt(ACC[:, :], ACC[:, :], SQ[:, u % 2, :], ALU.add).then_inc(sem("acc_done"), 1)

        def clear_acc():
            own.step(dve.memset(ACC[:, :], 0.0))

        clear_acc()
        residual(RUN_RWO, 1)
        lo_scaled(G_PE0, A_PE0)
        rstd(1)

        def embed(run, v, load):
            clear_acc()
            dve.wait_ge(sem("pp_in"), 16 * load)
            with dve.Fori(0, 2) as trip:
                own.enter(trip, 4)
                for u in range(4):
                    j = trip * 4 + u
                    got(run[1] + u, trip)
                    t = PTMP[:, u % 2, :]
                    tt(t, BANK[u], RB[:, :], ALU.mult).then_inc(sem("bank_free"), 1)
                    dve.wait_ge(sem("ple_gate"), trip * 4 + (NT * (load - 1) + u + 1))
                    own.step(tt(t, t, row(PP, j), ALU.mult))
                    tt(row(XT, j), row(XT, j), t, ALU.add).then_inc(sem("xt_done"), 1)
                    sum_tile(v, trip, u)
                own.leave(2)

        embed(RUN_PE0, 2, 1)
        dve.wait_ge(sem("da_in"), 96)
        LAM = STAT[:, 2, :]
        for n in range(2):
            own.step(tt(LQ[:, 2 * n, :], LQ[:, 2 * n, :], LQ[:, 2 * n + 1, :], ALU.mult))
            dve.tensor_reduce(LAM[:, n:n + 1], LQ[:, 2 * n, :], AX.X, ALU.add).then_inc(sem("lambda_sums"), 1)
        lo_scaled(G_DA, A_DA)
        dve.wait_ge(sem("lambda_exp"), 1)
        own.step(tt(LAM[:, 4:5], LAM[:, 3:4], LAM[:, 2:3], ALU.subtract))
        own.step(ts(LAM[:, 7:8], LAM[:, 4:5], -LAMBDA_INIT, None, ALU.add))
        own.step(dve.memset(LAM[:, 6:7], 1.0))
        rstd(2)
        for n in range(2):
            own.step(tt(ROPE[:, n, :], ROPE[:, n, :], RB[:, :], ALU.mult))
        for r, dst, k0 in ((RUN_DQ, DQT, 0), (RUN_DK, DKT, NT)):
            with dve.Fori(0, 2) as trip:
                own.enter(trip, 4)
                for u in range(4):
                    dve.wait_ge(sem("rotated"), trip * 4 + (k0 + u + 1))
                    tt(RTMP[:, 1, :], BANK[u], ROPE[:, 0, :], ALU.mult).then_inc(sem("bank_free"), 1)
                    own.step(tt(RTMP[:, 2, :], RTMP[:, 0, :], ROPE[:, 1, :], ALU.mult))
                    tt(row(dst, trip * 4 + u), RTMP[:, 1, :], RTMP[:, 2, :], ALU.add).then_inc(sem("rope_done"), 1)
                own.leave(2)
        with dve.Fori(0, 2) as trip:
            for u in range(4):
                got(RUN_DV[1] + u, trip)
                dve.wait_ge(sem("v_turned"), trip * 4 + (u + 1))
                tt(VSTAGE[:, u % 2, :], BANK[u], RB[:, :], ALU.mult).then_inc(sem("bank_free"), 1)
        with dve.Fori(0, 2) as trip:
            for u in range(4):
                got(RUN_DG[1] + u, trip)
                tt(row(DGT, trip * 4 + u), BANK[u], RB[:, :], ALU.mult).then_inc(sem("bank_free"), 1)
        mask = cst("causal_add").unsqueeze(1).to_broadcast([P, 2, P])
        with dve.Fori(0, NT // 2) as i:
            own.enter(i, 8 * 5)

            def maxima(s):
                q, par = s % TT, s % 2
                w = (q + 1) * P
                dve.wait_ge(sem("score_mm"), i * 8 + (s + 1))
                diag = PS[:, 2 * par:2 * par + 2, q * P:w]
                own.step(tt(diag, diag, mask, ALU.add))
                own.step(dve.tensor_reduce(STAT[:, par, 0:2], PS[:, 2 * par:2 * par + 2, 0:w], AX.X, ALU.max))
                ts(STAT[:, par, 2:4], STAT[:, par, 0:2], -QK_SCALE, None, ALU.mult).then_inc(sem("neg_max"), 1)

            def combine(s):
                par, w = s % 2, (s % TT + 1) * P
                dve.wait_ge(sem("exp_done"), i * 16 + (2 * s + 6))
                own.step(dve.reciprocal(STAT[:, par, 6:8], STAT[:, par, 4:6]))
                own.step(tt(STAT[:, par, 8:10], STAT[:, par, 6:8], LAM[:, 6:8], ALU.mult))
                own.step(ts(ES[:, par, 1, 0:w], ES[:, par, 1, 0:w], STAT[:, par, 9:10], None, ALU.mult))
                dve.wait_ge(sem("turn_mm"), i * 8 + (s + 1))
                stt(out=ATT[:, par, 0:w], in0=ES[:, par, 0, 0:w], scalar=STAT[:, par, 8:9], in1=ES[:, par, 1, 0:w],
                    op0=ALU.mult, op1=ALU.add).then_inc(sem("att_done"), 1)

            maxima(0)
            for s in range(8):
                if s < 7:
                    maxima(s + 1)
                combine(s)
                if s == 5:
                    dve.wait_ge(sem("value_mm"), i * 8 + (2 * TT + TT))
                    dve.tensor_copy(row(DQT, i * 2), BANK[6]).then_inc(sem("head_out"), 1)
            dve.wait_ge(sem("value_mm"), i * 8 + (2 * TT + 2 * TT))
            dve.tensor_copy(row(DQT, i * 2 + 1), BANK[7]).then_inc(sem("head_out"), 1)
            own.leave(NT // 2)
        dve.wait_ge(sem("sub_sqrt"), 1)
        dve.reciprocal(RK8[:, :], RK8[:, :]).then_inc(sem("sub_rstd"), 1)
        dve.wait_ge(sem("dg_done"), NT)
        for j in range(NT):
            dve.wait_ge(sem("sub_bcast"), j + 1)
            y = RTMP[:, j % 2, :]
            stt(out=y, in0=DQT[:, j, :], scalar=PRM[:, SUBLN * NT:SUBLN * NT + 1], in1=BANK[5 + j % 2],
                op0=ALU.mult, op1=ALU.mult).then_inc(sem("sub_scaled"), 1)
            dve.wait_ge(sem("sub_scaled"), j + 1)
            stt(out=DQT[:, j, :], in0=y, scalar=1.0 - LAMBDA_INIT, in1=DGT[:, j, :], op0=ALU.mult, op1=ALU.mult
                ).then_inc(sem("sub_done"), 1)
        lo_plain(lambda k: DQT[:, k, :], A_DAO)
        clear_acc()
        residual(RUN_DAO, 3)
        lo_scaled(G_PE1, A_PE1)
        rstd(3)
        embed(RUN_PE1, 4, 2)
        rstd(4)
        for j in range(NT):
            stt(out=XT[:, j, :], in0=XT[:, j, :], scalar=prm(G_FIRST, j), in1=RB[:, :], op0=ALU.mult, op1=ALU.mult
                ).then_inc(sem("xt_done"), 1)
            if j:
                accumulate(5, j - 1, j - 1)
        accumulate(5, NT - 1, NT - 1)
        lo_scaled(G_CONV, A_CONV)
        rstd(5)
        own.step(dve.memset(CU[:, :, 0:2], 0.0))
        with dve.Fori(0, 2) as trip:
            for u in range(4):
                got(RUN_CC[1] + u, trip)
                tt(CU[:, bass.ds(trip * 4 + u, 1), 2:TOK + 2], BANK[u], RB[:, :], ALU.mult).then_inc(sem("bank_free"), 1)
        dve.wait_ge(sem("bank_free"), RUN_CX[1])
        with dve.Fori(0, 2) as trip:
            own.enter(trip, 4 * 3)
            for u in range(4):
                j = trip * 4 + u
                x, y = CTMP[:, u % 2, :], row(CV, j)

                def tap(n, j=j):
                    return CU[:, bass.ds(j, 1), n:n + TOK]

                got(RUN_CX[1] + u, trip)
                tt(x, BANK[u], RB[:, :], ALU.mult).then_inc(sem("bank_free"), 1)
                dve.wait_ge(sem("bank_free"), trip * 4 + (RUN_CX[1] + u + 1))
                own.step(tt(tap(2), tap(2), x, ALU.mult))
                own.step(ts(y, tap(2), prm(CONV2, j), None, ALU.mult))
                own.step(stt(out=y, in0=tap(1), scalar=prm(CONV1, j), in1=y, op0=ALU.mult, op1=ALU.add))
                stt(out=y, in0=tap(0), scalar=prm(CONV0, j), in1=y, op0=ALU.mult, op1=ALU.add).then_inc(sem("taps_done"), 1)
            own.leave(2)
        dve.wait_ge(sem("taps_done"), NT)
        with dve.Fori(0, 2) as trip:
            for u in range(4):
                got(RUN_CB[1] + u, trip)
                x, y = CTMP[:, u % 2, :], row(CV, trip * 4 + u)
                tt(x, BANK[u], RB[:, :], ALU.mult).then_inc(sem("bank_free"), 1)
                dve.wait_ge(sem("bank_free"), trip * 4 + (RUN_CB[1] + u + 1))
                tt(y, y, x, ALU.mult).then_inc(sem("b_done"), 1)
        dve.wait_ge(sem("b_done"), NT)
        with dve.Fori(0, 2) as trip:
            for u in range(4):
                got(RUN_CG[1] + u, trip)
                x, y = CTMP[:, 2 + u % 2, :], row(CV, trip * 4 + u)
                tt(x, BANK[u], RB[:, :], ALU.mult).then_inc(sem("bank_free"), 1)
                dve.wait_ge(sem("cg_done"), trip * 4 + (u + 1))
                tt(y, y, x, ALU.mult).then_inc(sem("conv_done"), 1)
        lo_plain(lambda k: CV[:, k, :], A_CO)
        clear_acc()
        residual(RUN_CO, 6)
        lo_scaled(G_KV, A_KV)
        rstd(6)
        for u in range(HT4):
            got(RUN_KV[1] + u)
            tt(SKT[:, u, :], BANK[u], RB[:, :], ALU.mult).then_inc(sem("bank_free"), 1)
        for u in range(HT4):
            got(RUN_KV[1] + HT4 + u)
            dve.wait_ge(sem("sv_turned"), u + 1)
            tt(SVST[:, u % 2, :], BANK[u], RB[:, :], ALU.mult).then_inc(sem("bank_free"), 1)
        lo_scaled(G_B, A_QG)
        for u in range(HT4):
            got(RUN_QG[1] + u)
            stt(out=SQT[:, u, :], in0=BANK[u], scalar=QK_SCALE, in1=RB[:, :], op0=ALU.mult, op1=ALU.mult
                ).then_inc(sem("bank_free"), 1)
        for u in range(HT4):
            got(RUN_QG[1] + HT4 + u)
            tt(SGT[:, u, :], BANK[u], RB[:, :], ALU.mult).then_inc(sem("bank_free"), 1)
        dve.wait_ge(sem("sg_done"), HT4)
        NS = 2 * TT
        strict_mul = cst("strict_mul").unsqueeze(1).to_broadcast([P, 2, P])
        strict_add = cst("strict_add").unsqueeze(1).to_broadcast([P, 2, P])
        with dve.Fori(0, HT4 // 2) as i:
            own.enter(i, 3 * NS)

            def suffix_sums(s):
                q, par = s % TT, s % 2
                w = (q + 1) * P
                z, sp, suf = PS[:, 2 * par:2 * par + 2, 0:w], SSP[:, par, :, 0:w], SSUF[:, par, :, 0:w]
                dve.wait_ge(sem("ln_done"), i * NS + (s + 1))
                stt(out=sp, in0=z, scalar=0.0, in1=SAB[:, par, :, 0:w], op0=ALU.max, op1=ALU.add
                    ).then_inc(sem("sp_done"), 1)
                dve.wait_ge(sem("sp_done"), i * NS + (s + 3))
                own.step(tt(sp[:, :, q * P:w], sp[:, :, q * P:w], strict_mul, ALU.mult))
                dve.wait_ge(sem("weights_done"), i * NS + (s + 1))
                for h in range(2):
                    own.step(dve.tensor_tensor_scan(suf[:, h, ::-1], ONES[:, 0:1].to_broadcast([P, w]),
                                                    sp[:, h, ::-1], 0.0, ALU.mult, ALU.add))
                tt(suf, z, suf, ALU.subtract).then_inc(sem("z_free"), 1)
                dve.wait_ge(sem("z_free"), i * NS + (s + 3))
                tt(suf[:, :, q * P:w], suf[:, :, q * P:w], strict_add, ALU.add).then_inc(sem("log_weights"), 1)

            def keep_weights(s):
                w = (s % TT + 1) * P
                dve.wait_ge(sem("pair_mm"), i * NS + (s + 2 * TT - 1))
                for h in range(2):
                    dve.wait_ge(sem("wturn_mm"), i * 2 * NS + (2 * s + h + 5))
                    dve.tensor_copy(SATTT[:, s % 2, h, 0:w], BANK[4 + h][:, 0:w]).then_inc(sem("weights_turned"), 1)

            def pair(b):
                dve.wait_ge(sem("pair_mm"), i * NS + (2 * TT + TT * (b + 1)))
                j = i * 2 + b
                tt(row(SQT, j), BANK[6 + b], row(SGT, j), ALU.mult).then_inc(sem("pair_out"), 1)

            for s in range(NS):
                suffix_sums(s)
                if s:
                    keep_weights(s - 1)
                if s == TT + 1:
                    pair(0)
            keep_weights(NS - 1)
            pair(1)
            own.leave(HT4 // 2)
        lo_plain(lambda k: SQT[:, k, :], A_BO, HT4)
        for n in range(NT):
            got(RUN_BO[1] + n)
            tt(XT[:, n, :], XT[:, n, :], BANK[n % 4], ALU.add).then_inc(sem("xt_done"), 1)
            dve.wait_ge(sem("xt_done"), NT * 7 + n + 1)
            dve.sem_inc(sem("bank_free"), 1)
            accumulate(7, n, n)
        rstd(7)
        for j in range(NT):
            if j >= 2:
                dve.wait_ge(sem("final_mm"), j - 1)
            stt(out=FT[:, j % 2, :], in0=XT[:, j, :], scalar=prm(G_LAST, j), in1=RB[:, :], op0=ALU.mult, op1=ALU.mult
                ).then_inc(sem("final_scaled"), 1)


INPUTS = ["x", "p", "rw_norm", "rw_mu", "rw_w_in", "rw_w0", "rw_w1", "rw_w2", "rw_a0", "rw_a1", "rw_a2", "rw_k_k",
          "rw_k_a", "rw_r_k", "rw_ln_w", "rw_ln_b", "rw_w_out", "da_norm", "da_w_in", "da_lq1", "da_lk1", "da_lq2",
          "da_lk2", "da_subln", "da_w_out", "pe_norm", "pe_w_gate", "pe_w_proj", "final_norm", "norm_a_2",
          "w_in_a_2", "conv_a_2", "w_out_a_2", "norm_kv_2", "w_kv_2", "norm_b_2", "w_in_b_2", "w_out_b_2", "norm_f_2"]


def kernel(**inputs):
    import concourse.bacc as bacc
    from concourse.bass_utils import run_bass_kernel_spmd

    nc = bacc.Bacc("TRN2", target_bir_lowering=False, num_devices=1)
    arrays = {name: np.ascontiguousarray(inputs[name]) for name in INPUTS}
    arrays.update(constant_tables())
    a = {name: nc.dram_tensor(name, x.shape, mybir.dt.from_np(x.dtype), kind="ExternalInput").ap()
         for name, x in arrays.items()}
    out = nc.dram_tensor("out", (1, TOK, DM), F32, kind="ExternalOutput").ap()
    build(nc, a, out)
    result = run_bass_kernel_spmd(nc, [arrays], core_ids=[0])
    return result.results[0]["out"]
```
